# Optimizing a Trainium2 kernel written in Bass

```python
import math
import jax, jax.numpy as jnp
from jax import lax
import numpy as np
import jax
import jax.numpy as jnp

D_MODEL = 1024
BATCH = 1
SEQ = 256
DEPTH = 2

N_A = DEPTH // 2
N_B = DEPTH - N_A
CONV_WIDTH = 31
FFN_CONV_WIDTH = 3
D_FF = 2816
N_HEADS = 8
HEAD_DIM = D_MODEL // N_HEADS
WINDOWS = (128, 512, 2048)
DILATIONS = (1, 4, 16)
N_GROUPS = len(WINDOWS)
Q_WIDTH = N_GROUPS * N_HEADS * HEAD_DIM
BLOCK = 128
EPS = 1e-6
NEG_INF = -1e30


def rms_norm(x, g):
    xf = x.astype(jnp.float32)
    y = xf * lax.rsqrt(jnp.mean(xf * xf, axis=-1, keepdims=True) + EPS)
    return (y * g.astype(jnp.float32)).astype(x.dtype)

def layer_norm(x, g, b):
    xf = x.astype(jnp.float32)
    mu = jnp.mean(xf, axis=-1, keepdims=True)
    var = jnp.mean(jnp.square(xf - mu), axis=-1, keepdims=True)
    y = (xf - mu) * lax.rsqrt(var + EPS)
    return (y * g.astype(jnp.float32) + b.astype(jnp.float32)).astype(x.dtype)

def causal_dwconv(x, w, b):
    k, c = w.shape
    y = lax.conv_general_dilated(
        x, w[:, None, :].astype(x.dtype), window_strides=(1,), padding=[(k - 1, 0)],
        dimension_numbers=("NWC", "WIO", "NWC"), feature_group_count=c)
    return y + b

def conformer_conv_module(h, w_in, b_in, dw, dw_b, ln_g, ln_b, w_out, b_out):
    u = h @ w_in + b_in
    u = u[..., :D_MODEL] * jax.nn.sigmoid(u[..., D_MODEL:])
    u = causal_dwconv(u, dw, dw_b)
    u = layer_norm(u, ln_g, ln_b)
    u = jax.nn.silu(u)
    return u @ w_out + b_out

def conv_ffn(h, w_in, dw, dw_b, w_out):
    u = causal_dwconv(h @ w_in, dw, dw_b)
    a, g = u[..., :D_FF], u[..., D_FF:]
    return (jax.nn.silu(g) * a) @ w_out

def dilated_branch(q, k, v, window, dil):
    b, s, h, dh = q.shape
    steps = window // dil
    assert steps <= BLOCK and s % dil == 0
    L = s // dil
    nblk = -(-L // BLOCK)
    lp = nblk * BLOCK

    def to_sub(t):
        t = t.reshape(b, L, dil, h, dh).transpose(0, 2, 3, 1, 4)
        return jnp.pad(t, ((0, 0), (0, 0), (0, 0), (0, lp - L), (0, 0)))

    qs, ks, vs = to_sub(q), to_sub(k), to_sub(v)
    q_blk = qs.reshape(b, dil, h, nblk, BLOCK, dh)

    def band(t):
        tp = jnp.pad(t, ((0, 0), (0, 0), (0, 0), (BLOCK, 0), (0, 0)))
        prev = tp[:, :, :, :lp].reshape(b, dil, h, nblk, BLOCK, dh)
        cur = tp[:, :, :, BLOCK:].reshape(b, dil, h, nblk, BLOCK, dh)
        return jnp.concatenate([prev, cur], axis=-2)

    k_band, v_band = band(ks), band(vs)
    scores = jnp.einsum("brhnqc,brhnkc->brhnqk", q_blk, k_band).astype(jnp.float32)
    scores = scores * (1.0 / math.sqrt(dh))

    blk_i = jnp.arange(nblk)[:, None, None]
    qi = jnp.arange(BLOCK)[None, :, None]
    kk = jnp.arange(2 * BLOCK)[None, None, :]
    dist = qi + BLOCK - kk
    key_pos = blk_i * BLOCK + kk - BLOCK
    valid = (dist >= 0) & (dist <= steps) & (key_pos >= 0)
    scores = jnp.where(valid, scores, NEG_INF)

    m = jnp.max(scores, axis=-1, keepdims=True)
    p = jnp.exp(scores - m)
    den = jnp.sum(p, axis=-1, keepdims=True)
    out = jnp.einsum("brhnqk,brhnkc->brhnqc", p.astype(v.dtype), v_band)
    out = out / den.astype(out.dtype)
    lse = (m + jnp.log(den))[..., 0]

    out = out.reshape(b, dil, h, lp, dh)[:, :, :, :L]
    out = out.transpose(0, 3, 1, 2, 4).reshape(b, s, h, dh)
    lse = lse.reshape(b, dil, h, lp)[:, :, :, :L]
    lse = lse.transpose(0, 3, 1, 2).reshape(b, s, h)
    return out, lse

def dilated_mixture_attention(h, w_q, w_o, k, v):
    b, s, _ = h.shape
    q = (h @ w_q).reshape(b, s, N_GROUPS, N_HEADS, HEAD_DIM)
    outs, lses = [], []
    for g in range(N_GROUPS):
        o, l = dilated_branch(q[:, :, g], k[:, :, g], v[:, :, g], WINDOWS[g], DILATIONS[g])
        outs.append(o)
        lses.append(l)
    outs = jnp.stack(outs, axis=0)
    wts = jax.nn.softmax(jnp.stack(lses, axis=0), axis=0)
    merged = jnp.sum(wts[..., None].astype(outs.dtype) * outs, axis=0)
    return merged.reshape(b, s, N_HEADS * HEAD_DIM) @ w_o

def first_inputs(seed: int = 0) -> dict:
    key = jax.random.key(seed)
    ks = iter(jax.random.split(key, 32))

    def nrm(shape, fan_in):
        return jax.random.normal(next(ks), shape, jnp.float32) * (fan_in ** -0.5)

    def gain(shape):
        return 1.0 + 0.02 * jax.random.normal(next(ks), shape, jnp.float32)

    def bias(shape):
        return 0.01 * jax.random.normal(next(ks), shape, jnp.float32)

    d = D_MODEL
    return {
        "x": jax.random.normal(next(ks), (BATCH, SEQ, d), jnp.float32),
        "mix_pre_g": gain((DEPTH, d)),
        "mix_post_g": gain((DEPTH, d)),
        "ffn_pre_g": gain((DEPTH, d)),
        "ffn_post_g": gain((DEPTH, d)),
        "cm_w_in": nrm((N_A, d, 2 * d), d),
        "cm_b_in": bias((N_A, 2 * d)),
        "cm_dw": nrm((N_A, CONV_WIDTH, d), CONV_WIDTH),
        "cm_dw_b": bias((N_A, d)),
        "cm_ln_g": gain((N_A, d)),
        "cm_ln_b": bias((N_A, d)),
        "cm_w_out": nrm((N_A, d, d), d),
        "cm_b_out": bias((N_A, d)),
        "kv_norm_g": gain((d,)),
        "w_kv": nrm((d, 2 * Q_WIDTH), d),
        "w_q": nrm((N_B, d, Q_WIDTH), d),
        "w_o": nrm((N_B, N_HEADS * HEAD_DIM, d), N_HEADS * HEAD_DIM),
        "ffn_w_in": nrm((DEPTH, d, 2 * D_FF), d),
        "ffn_dw": nrm((DEPTH, FFN_CONV_WIDTH, 2 * D_FF), FFN_CONV_WIDTH),
        "ffn_dw_b": bias((DEPTH, 2 * D_FF)),
        "ffn_w_out": nrm((DEPTH, D_FF, d), D_FF),
    }

def first_block(x, mix_pre_g, mix_post_g, ffn_pre_g, ffn_post_g,
              cm_w_in, cm_b_in, cm_dw, cm_dw_b, cm_ln_g, cm_ln_b, cm_w_out, cm_b_out,
              kv_norm_g, w_kv, w_q, w_o,
              ffn_w_in, ffn_dw, ffn_dw_b, ffn_w_out):
    b, s, _ = x.shape
    k_sh = v_sh = None
    for i in range(DEPTH):
        h = rms_norm(x, mix_pre_g[i])
        if i < N_A:
            y = conformer_conv_module(h, cm_w_in[i], cm_b_in[i], cm_dw[i], cm_dw_b[i],
                                      cm_ln_g[i], cm_ln_b[i], cm_w_out[i], cm_b_out[i])
        else:
            j = i - N_A
            y = dilated_mixture_attention(h, w_q[j], w_o[j], k_sh, v_sh)
        x = x + rms_norm(y, mix_post_g[i])
        h = rms_norm(x, ffn_pre_g[i])
        y = conv_ffn(h, ffn_w_in[i], ffn_dw[i], ffn_dw_b[i], ffn_w_out[i])
        x = x + rms_norm(y, ffn_post_g[i])
        if i == N_A - 1:
            kv = (rms_norm(x, kv_norm_g) @ w_kv).reshape(b, s, 2, N_GROUPS, N_HEADS, HEAD_DIM)
            k_sh, v_sh = kv[:, :, 0], kv[:, :, 1]
    return x


DEPTH_2 = 1

GRID_W = 64
CTX_LEN = 256
NH_M = 4
DQK_M = D_MODEL // 8
DV_M = D_MODEL // 4
MLSTM_CHUNK = 128
NH_D = 8
DH_D = D_MODEL // 16
Q_BLOCK = 128
ROPE_BASE = 10000.0
N_EXPERTS = 32
TOP_K = 4
D_FF_2 = D_MODEL
SWIGLU_LIMIT = 7.0
SWIGLU_ALPHA = 1.702
EXPERT_BLOCK = 128
NORM_EPS = 1e-6
SPLIT_SIZES = (NH_M * DQK_M, NH_M * DQK_M, NH_M * DV_M, 4 * NH_M, NH_M * DV_M,
               NH_D * 2 * DH_D, NH_D * 2 * DH_D, NH_D * 2 * DH_D, D_MODEL, D_MODEL)
IN_COLS = sum(SPLIT_SIZES)


def rmsnorm(x, g):
    xf = x.astype(jnp.float32)
    y = xf * lax.rsqrt(jnp.mean(xf * xf, axis=-1, keepdims=True) + NORM_EPS)
    return (y * g.astype(jnp.float32)).astype(x.dtype)

def modulate(u, shift, scale):
    return u * (1 + scale) + shift

def split_proj(u, w_in):
    return jnp.split(u @ w_in, np.cumsum(SPLIT_SIZES)[:-1].tolist(), axis=-1)

def axial_rope_tables(n_tok):
    rows = n_tok // GRID_W
    row = jnp.repeat(jnp.arange(rows, dtype=jnp.float32), GRID_W)
    col = jnp.tile(jnp.arange(GRID_W, dtype=jnp.float32), rows)
    n_freq = DH_D // 4
    inv_freq = ROPE_BASE ** (-jnp.arange(n_freq, dtype=jnp.float32) / n_freq)
    ang_r = (row[:, None] * inv_freq)[:, None, None, :]
    ang_c = (col[:, None] * inv_freq)[:, None, None, :]
    return (jnp.cos(ang_r), jnp.sin(ang_r), jnp.cos(ang_c), jnp.sin(ang_c))

def rotate_pairs(x, cos, sin):
    x1, x2 = jnp.split(x, 2, axis=-1)
    cos = cos.astype(x.dtype)
    sin = sin.astype(x.dtype)
    return jnp.concatenate([x1 * cos - x2 * sin, x2 * cos + x1 * sin], axis=-1)

def apply_axial_rope(x, tables):
    cos_r, sin_r, cos_c, sin_c = tables
    half = DH_D // 2
    return jnp.concatenate([rotate_pairs(x[..., :half], cos_r, sin_r),
                            rotate_pairs(x[..., half:], cos_c, sin_c)], axis=-1)

def mlstm_chunkwise(q, k, v, i_pre, logf, state):
    b_, h_, t_, _ = q.shape
    L = MLSTM_CHUNK
    nc = t_ // L

    def chunks(a):
        return jnp.moveaxis(a.reshape(a.shape[:2] + (nc, L) + a.shape[3:]), 2, 0)

    causal = jnp.tril(jnp.ones((L, L), dtype=bool))

    def step(carry, xs):
        C, n, m = carry
        qc, kc, vc, ic, fc = xs
        bcum = jnp.cumsum(fc, axis=-1)
        log_d = jnp.where(causal, bcum[..., :, None] - bcum[..., None, :] + ic[..., None, :], -jnp.inf)
        inter = bcum + m[..., None]
        m_t = jnp.maximum(inter, jnp.max(log_d, axis=-1))
        s = jnp.einsum('bhtk,bhsk->bhts', qc, kc) * jnp.exp(log_d - m_t[..., None])
        w_inter = jnp.exp(inter - m_t)
        num = w_inter[..., None] * jnp.einsum('bhtk,bhkv->bhtv', qc, C) + jnp.einsum('bhts,bhsv->bhtv', s, vc)
        den = w_inter * jnp.einsum('bhtk,bhk->bht', qc, n) + jnp.sum(s, axis=-1)
        h = num / jnp.maximum(jnp.abs(den), jnp.exp(-m_t))[..., None]
        b_last = bcum[..., -1]
        log_w = b_last[..., None] - bcum + ic
        m_new = jnp.maximum(b_last + m, jnp.max(log_w, axis=-1))
        w = jnp.exp(log_w - m_new[..., None])
        decay = jnp.exp(b_last + m - m_new)
        C_new = decay[..., None, None] * C + jnp.einsum('bhsk,bhsv->bhkv', kc * w[..., None], vc)
        n_new = decay[..., None] * n + jnp.einsum('bhs,bhsk->bhk', w, kc)
        return (C_new, n_new, m_new), h

    state, h = lax.scan(step, state, (chunks(q), chunks(k), chunks(v), chunks(i_pre), chunks(logf)))
    return jnp.moveaxis(h, 0, 2).reshape(b_, h_, t_, v.shape[-1]), state

def mlstm_zero_state(batch):
    return (jnp.zeros((batch, NH_M, DQK_M, DV_M), jnp.float32),
            jnp.zeros((batch, NH_M, DQK_M), jnp.float32),
            jnp.zeros((batch, NH_M), jnp.float32))

def mlstm_prepare(p, gate_b):
    b, t = p[0].shape[:2]

    def heads(a, d):
        return a.reshape(b, t, NH_M, d).transpose(0, 2, 1, 3).astype(jnp.float32)

    q = heads(p[0], DQK_M) * DQK_M ** -0.5
    k = heads(p[1], DQK_M)
    v = heads(p[2], DV_M)
    g = (p[3] + gate_b).astype(jnp.float32).reshape(b, t, 4, NH_M).transpose(2, 0, 3, 1)
    return q, k, v, g

def mlstm_direction(q, k, v, i_pre, f_pre, state, reverse):
    logf = jax.nn.log_sigmoid(f_pre)
    if reverse:
        q, k, v, i_pre, logf = (jnp.flip(a, axis=2) for a in (q, k, v, i_pre, logf))
    h, state = mlstm_chunkwise(q, k, v, i_pre, logf, state)
    if reverse:
        h = jnp.flip(h, axis=2)
    return h, state

def mlstm_output(h, o_raw, g):
    b, t = o_raw.shape[:2]
    hn = rmsnorm(h.transpose(0, 2, 1, 3), g)
    o = jax.nn.sigmoid(o_raw.astype(jnp.float32)).reshape(b, t, NH_M, DV_M)
    return (hn * o).reshape(b, t, NH_M * DV_M).astype(o_raw.dtype)

def diff_prepare(p, tables):
    b, t = p[5].shape[:2]
    q = p[5].reshape(b, t, NH_D, 2, DH_D)
    k = p[6].reshape(b, t, NH_D, 2, DH_D)
    if tables is not None:
        q = apply_axial_rope(q, tables)
        k = apply_axial_rope(k, tables)
    v = p[7].reshape(b, t, NH_D, 2 * DH_D)
    return q.transpose(0, 2, 3, 1, 4), k.transpose(0, 2, 3, 1, 4), v.transpose(0, 2, 1, 3)

def diff_attend(q, k, v, lam):
    s = jnp.einsum('bhmqd,bhmkd->bhmqk', q, k).astype(jnp.float32) * DH_D ** -0.5
    p = jax.nn.softmax(s, axis=-1)
    a = p[:, :, 0] - lam * p[:, :, 1]
    return jnp.einsum('bhqk,bhkd->bhqd', a.astype(v.dtype), v)

def diff_output(o, g, lam_init):
    b, h, t, d = o.shape
    on = rmsnorm(o.transpose(0, 2, 1, 3), g) * (1.0 - lam_init)
    return on.reshape(b, t, h * d)

def merge_branches(p, a_out, b_out, w_a, w_b, w_o):
    y = jax.nn.sigmoid(p[8]) * (a_out @ w_a) + jax.nn.sigmoid(p[9]) * (b_out @ w_b)
    return y @ w_o

def token_mixer(u, uc, tables, w_in, gate_b, m_norm_g, lam_p, d_norm_g, w_a, w_b, w_o, lam_init, need_ctx):
    pl = split_proj(u, w_in)
    pc = split_proj(uc, w_in)
    ql, kl, vl, gl = mlstm_prepare(pl, gate_b)
    qc, kc, vc, gc = mlstm_prepare(pc, gate_b)
    st0 = mlstm_zero_state(uc.shape[0])
    h_cf, st_f = mlstm_direction(qc, kc, vc, gc[0], gc[1], st0, False)
    h_cb, st_b = mlstm_direction(qc, kc, vc, gc[2], gc[3], st0, True)
    h_lf, _ = mlstm_direction(ql, kl, vl, gl[0], gl[1], st_f, False)
    h_lb, _ = mlstm_direction(ql, kl, vl, gl[2], gl[3], st_b, True)
    a_lat = mlstm_output(h_lf + h_lb, pl[4], m_norm_g)
    lp = lam_p.astype(jnp.float32)
    lam = jnp.exp(jnp.sum(lp[0] * lp[1])) - jnp.exp(jnp.sum(lp[2] * lp[3])) + lam_init
    qdl, kdl, vdl = diff_prepare(pl, tables)
    qdc, kdc, vdc = diff_prepare(pc, None)
    k_all = jnp.concatenate([kdc, kdl], axis=3)
    v_all = jnp.concatenate([vdc, vdl], axis=2)
    b, h, _, t, dh = qdl.shape
    n_blk = t // Q_BLOCK
    q_blocks = jnp.moveaxis(qdl.reshape(b, h, 2, n_blk, Q_BLOCK, dh), 3, 0)
    o_blocks = lax.map(lambda qb: diff_attend(qb, k_all, v_all, lam), q_blocks)
    o_lat = jnp.moveaxis(o_blocks, 0, 2).reshape(b, h, t, 2 * dh)
    b_lat = diff_output(o_lat, d_norm_g, lam_init)
    y = merge_branches(pl, a_lat, b_lat, w_a, w_b, w_o)
    if not need_ctx:
        return y, None
    a_ctx = mlstm_output(h_cf + h_cb, pc[4], m_norm_g)
    b_ctx = diff_output(diff_attend(qdc, kdc, vdc, lam), d_norm_g, lam_init)
    return y, merge_branches(pc, a_ctx, b_ctx, w_a, w_b, w_o)

def moe_ffn(u, router_w, router_b, w1, b1, w2, b2):
    b, t, d = u.shape
    n_tok = b * t
    xf = u.reshape(n_tok, d)
    logits = (xf @ router_w + router_b).astype(jnp.float32)
    top_val, top_idx = lax.top_k(logits, TOP_K)
    gate = jax.nn.softmax(top_val, axis=-1).astype(u.dtype)
    n_asg = n_tok * TOP_K
    flat_e = top_idx.reshape(n_asg)
    flat_tok = jnp.arange(n_asg, dtype=jnp.int32) // TOP_K
    order = jnp.argsort(flat_e)
    sorted_e = flat_e[order]
    counts = jnp.bincount(flat_e, length=N_EXPERTS)
    padded = (counts + EXPERT_BLOCK - 1) // EXPERT_BLOCK * EXPERT_BLOCK
    pad_end = jnp.cumsum(padded)
    pad_start = pad_end - padded
    sorted_start = jnp.cumsum(counts) - counts
    dest = pad_start[sorted_e] + jnp.arange(n_asg) - sorted_start[sorted_e]
    n_buf = -(-n_asg // EXPERT_BLOCK) * EXPERT_BLOCK + N_EXPERTS * EXPERT_BLOCK
    buf_tok = jnp.zeros((n_buf,), jnp.int32).at[dest].set(flat_tok[order])
    buf_w = jnp.zeros((n_buf,), u.dtype).at[dest].set(gate.reshape(n_asg)[order])
    n_blk = n_buf // EXPERT_BLOCK
    blk_e = jnp.minimum(jnp.searchsorted(pad_end, jnp.arange(n_blk) * EXPERT_BLOCK, side='right'), N_EXPERTS - 1)

    def expert_block(args):
        tok, e = args
        hcat = xf[tok] @ w1[e] + b1[e]
        h_glu = jnp.minimum(hcat[:, :D_FF_2], SWIGLU_LIMIT)
        h_lin = jnp.clip(hcat[:, D_FF_2:], -SWIGLU_LIMIT, SWIGLU_LIMIT)
        act = h_glu * jax.nn.sigmoid(SWIGLU_ALPHA * h_glu) * (h_lin + 1)
        return act @ w2[e] + b2[e]

    y_buf = lax.map(expert_block, (buf_tok.reshape(n_blk, EXPERT_BLOCK), blk_e))
    y = jax.ops.segment_sum(y_buf.reshape(n_buf, d) * buf_w[:, None], buf_tok, num_segments=n_tok)
    return y.reshape(b, t, d)

def second_inputs(seed: int = 0) -> dict:
    key = jax.random.key(seed)
    ks = jax.random.split(key, 24)

    def nrm(k, shape, scale):
        return jax.random.normal(k, shape, jnp.float32) * scale

    L = DEPTH_2
    gate_base = jnp.array([0.0, 3.0, 0.0, 3.0], jnp.float32)[None, :, None]
    return {
        'x': nrm(ks[0], (BATCH, SEQ, D_MODEL), 1.0),
        'c': nrm(ks[1], (BATCH, D_MODEL), 1.0),
        'ctx': nrm(ks[2], (BATCH, CTX_LEN, D_MODEL), 1.0),
        'c_ctx': nrm(ks[3], (D_MODEL,), 1.0),
        'ada_w': nrm(ks[4], (L, D_MODEL, 6 * D_MODEL), 0.5 * D_MODEL ** -0.5),
        'ada_b': nrm(ks[5], (L, 6 * D_MODEL), 0.02),
        'norm1_g': 1.0 + nrm(ks[6], (L, D_MODEL), 0.02),
        'norm2_g': 1.0 + nrm(ks[7], (L, D_MODEL), 0.02),
        'w_in': nrm(ks[8], (L, D_MODEL, IN_COLS), D_MODEL ** -0.5),
        'mlstm_gate_b': (gate_base + nrm(ks[9], (L, 4, NH_M), 0.1)).reshape(L, 4 * NH_M),
        'mlstm_norm_g': 1.0 + nrm(ks[10], (L, NH_M, DV_M), 0.02),
        'diff_lambda': nrm(ks[11], (L, 4, DH_D), 0.1),
        'diff_norm_g': 1.0 + nrm(ks[12], (L, NH_D, 2 * DH_D), 0.02),
        'w_branch_a': nrm(ks[13], (L, NH_M * DV_M, D_MODEL), (NH_M * DV_M) ** -0.5),
        'w_branch_b': nrm(ks[14], (L, NH_D * 2 * DH_D, D_MODEL), (NH_D * 2 * DH_D) ** -0.5),
        'w_out': nrm(ks[15], (L, D_MODEL, D_MODEL), D_MODEL ** -0.5),
        'router_w': nrm(ks[16], (L, D_MODEL, N_EXPERTS), D_MODEL ** -0.5),
        'router_b': nrm(ks[17], (L, N_EXPERTS), 0.01),
        'exp_w1': nrm(ks[18], (L, N_EXPERTS, D_MODEL, 2 * D_FF_2), D_MODEL ** -0.5),
        'exp_b1': nrm(ks[19], (L, N_EXPERTS, 2 * D_FF_2), 0.01),
        'exp_w2': nrm(ks[20], (L, N_EXPERTS, D_FF_2, D_MODEL), D_FF_2 ** -0.5),
        'exp_b2': nrm(ks[21], (L, N_EXPERTS, D_MODEL), 0.01),
        'final_norm_g': 1.0 + nrm(ks[22], (D_MODEL,), 0.02),
    }

def second_block(x, c, ctx, c_ctx, ada_w, ada_b, norm1_g, norm2_g, w_in, mlstm_gate_b, mlstm_norm_g,
              diff_lambda, diff_norm_g, w_branch_a, w_branch_b, w_out, router_w, router_b,
              exp_w1, exp_b1, exp_w2, exp_b2, final_norm_g):
    tables = axial_rope_tables(x.shape[1])
    xc = ctx
    for l in range(DEPTH_2):
        need_ctx = l < DEPTH_2 - 1
        lam_init = 0.8 - 0.6 * math.exp(-0.3 * l)
        mod = jax.nn.silu(c) @ ada_w[l] + ada_b[l]
        sh1, sc1, g1, sh2, sc2, g2 = jnp.split(mod[:, None, :], 6, axis=-1)
        modc = jax.nn.silu(c_ctx) @ ada_w[l] + ada_b[l]
        sh1c, sc1c, g1c, sh2c, sc2c, g2c = jnp.split(modc, 6, axis=-1)
        u = modulate(rmsnorm(x, norm1_g[l]), sh1, sc1)
        uc = modulate(rmsnorm(xc, norm1_g[l]), sh1c, sc1c)
        y, yc = token_mixer(u, uc, tables, w_in[l], mlstm_gate_b[l], mlstm_norm_g[l], diff_lambda[l],
                            diff_norm_g[l], w_branch_a[l], w_branch_b[l], w_out[l], lam_init, need_ctx)
        x = x + g1 * y
        x = x + g2 * moe_ffn(modulate(rmsnorm(x, norm2_g[l]), sh2, sc2), router_w[l], router_b[l],
                             exp_w1[l], exp_b1[l], exp_w2[l], exp_b2[l])
        if need_ctx:
            xc = xc + g1c * yc
            xc = xc + g2c * moe_ffn(modulate(rmsnorm(xc, norm2_g[l]), sh2c, sc2c), router_w[l], router_b[l],
                                    exp_w1[l], exp_b1[l], exp_w2[l], exp_b2[l])
    return rmsnorm(x, final_norm_g)


def setup_inputs(seed=0):
    out = dict(first_inputs(seed))
    for name, value in second_inputs(seed + 1).items():
        if name != "x":
            out[name + "_2"] = value
    return out


def reference(
    x, mix_pre_g, mix_post_g, ffn_pre_g, ffn_post_g, cm_w_in, cm_b_in, cm_dw, cm_dw_b, cm_ln_g,
    cm_ln_b, cm_w_out, cm_b_out, kv_norm_g, w_kv, w_q, w_o, ffn_w_in, ffn_dw, ffn_dw_b,
    ffn_w_out, c_2, ctx_2, c_ctx_2, ada_w_2, ada_b_2, norm1_g_2, norm2_g_2, w_in_2,
    mlstm_gate_b_2, mlstm_norm_g_2, diff_lambda_2, diff_norm_g_2, w_branch_a_2, w_branch_b_2,
    w_out_2, router_w_2, router_b_2, exp_w1_2, exp_b1_2, exp_w2_2, exp_b2_2, final_norm_g_2,
):
    x = first_block(
        x, mix_pre_g, mix_post_g, ffn_pre_g, ffn_post_g, cm_w_in, cm_b_in, cm_dw, cm_dw_b,
        cm_ln_g, cm_ln_b, cm_w_out, cm_b_out, kv_norm_g, w_kv, w_q, w_o, ffn_w_in, ffn_dw,
        ffn_dw_b, ffn_w_out,
    )
    return second_block(
        x, c_2, ctx_2, c_ctx_2, ada_w_2, ada_b_2, norm1_g_2, norm2_g_2, w_in_2, mlstm_gate_b_2,
        mlstm_norm_g_2, diff_lambda_2, diff_norm_g_2, w_branch_a_2, w_branch_b_2, w_out_2,
        router_w_2, router_b_2, exp_w1_2, exp_b1_2, exp_w2_2, exp_b2_2, final_norm_g_2,
    )


_drawn_inputs = setup_inputs


def setup_inputs(seed=0):
    import zlib

    import numpy as np

    out = dict(_drawn_inputs(seed))
    spreads = {}
    factors = {'ffn_post_g': 3.363,
     'cm_b_in': 4.267,
     'cm_ln_b': 4.022,
     'kv_norm_g': 3.891,
     'ffn_dw_b': 4.194,
     'ctx_2': 2.962,
     'ada_b_2': 4.351,
     'norm1_g_2': 8.0,
     'norm2_g_2': 8.0,
     'mlstm_gate_b_2': 2.883,
     'mlstm_norm_g_2': 121.211,
     'diff_lambda_2': 8.0,
     'diff_norm_g_2': 40.819,
     'router_b_2': 36.247,
     'exp_b1_2': 38.282,
     'exp_b2_2': 200.0,
     'final_norm_g_2': 26.968}
    for name, (base, spread) in spreads.items():
        noise = np.random.default_rng([zlib.crc32(name.encode()), seed]).standard_normal(out[name].shape)
        drawn = base * np.exp(spread * noise) if base else spread * noise
        out[name] = jnp.asarray(drawn.astype(out[name].dtype))
    for name, factor in factors.items():
        out[name] = (out[name] * factor).astype(out[name].dtype)
    return out
```

```python
from contextlib import ExitStack

import numpy as np

import concourse.bass as bass
from concourse import mybir

P = 128
T = 256
D = 1024
KT = D // P
D_FF = 2816
FT = D_FF // P
TAPS = 31
GROUPS = 3
HEADS = 8
EXPERTS = 32
TOP_K = 4
CAP = 64
PAIRS = EXPERTS // 2
SLAB = 2048
RING = 8
EXPERT_RING = 12
UNIT_BANKS = 3
STAT = 3
WORK = 4
EPS = 1e-6
NEG = -1e30
SCALE_A = float(128 ** -0.5)
SCALE_M = float(128 ** -0.5)
SCALE_D = float(64 ** -0.5)
LAM_INIT = 0.8 - 0.6

F32 = mybir.dt.float32
I32 = mybir.dt.int32
ALU = mybir.AluOpType
ACT = mybir.ActivationFunctionType
AX = mybir.AxisListType

SCHEDULE = [
    ("ada0", 2, 1), ("cm_in", 8, 8), ("ada1", 2, 1), ("cm_out", 4, 4), ("ada2", 2, 1),
    ("ffn0_in", 22, 22), ("ffn0_out", 11, 0), ("ada3", 2, 1),
    ("kv", 24, 24), ("q", 12, 12), ("ada4", 2, 1), ("o", 4, 4), ("ada5", 2, 1),
    ("ffn1_in", 22, 22), ("ffn1_out", 11, 0),
    ("mq", 2, 2), ("mk", 2, 4), ("mv", 4, 8),
    ("dq", 4, 4), ("dk", 4, 8), ("dv", 4, 8), ("ada6", 12, 6),
    ("go", 4, 4), ("ga", 4, 4), ("gb", 4, 4),
    ("wa", 4, 4), ("wb", 4, 4), ("wo", 4, 4),
]
FIRST_SLAB, FIRST_UNIT, SLABS_OF, UNITS_OF = {}, {}, {}, {}
_g = _u = 0
for _n, _k, _w in SCHEDULE:
    FIRST_SLAB[_n], FIRST_UNIT[_n], SLABS_OF[_n], UNITS_OF[_n] = _g, _u, _k, _w
    _g += _k
    _u += _w
DENSE_SLABS, UNITS = _g, _u

PARAMS = [("mix_pre", 16), ("mix_post", 16), ("ffn_pre", 16), ("ffn_post", 16), ("cm_b_in", 16),
          ("cm_dw", TAPS * 8), ("cm_dw_b", 8), ("cm_ln_g", 8), ("cm_ln_b", 8), ("cm_b_out", 8),
          ("kv_norm", 8), ("ffn_dw", 2 * 3 * 44), ("ffn_dw_b", 2 * 44),
          ("c", 8), ("c_ctx", 8), ("ada_b", 48), ("norm1", 8), ("norm2", 8), ("m_norm", 8),
          ("d_norm", 8), ("final", 8)]
PAR, _g = {}, 0
for _n, _k in PARAMS:
    PAR[_n] = _g
    _g += _k
NPAR = _g

CONSTS = [("ident", 128), ("ones", 128), ("mean1024", 128), ("mean256", 128), ("mean128", 128),
          ("upto", 128), ("before", 128), ("from_", 128), ("rot", 128), ("cos", 256), ("sin", 256),
          ("slot", CAP), ("mask", 1152), ("lower", 128), ("upper", 128)]
CON, _g = {}, 0
for _n, _k in CONSTS:
    CON[_n] = _g
    _g += _k
NCON = _g

ROWS = {"lam": 0, "gate_b": 256, "router_b": 272}
NROW = 272 + EXPERTS


def mlstm_masks():
    q = np.arange(T).reshape(2, P)[:, :, None]
    k = np.arange(T)[None, None, :]
    ok = np.stack([k <= q, k >= q], 1)
    out = np.concatenate([np.zeros((2, 2, P, T)), np.where(ok, 0.0, NEG)], 3)
    return np.ascontiguousarray(out.transpose(2, 0, 1, 3).reshape(P, 2048).astype(np.float32))


def constants():
    i, j = np.arange(P)[:, None], np.arange(P)[None, :]
    out = np.zeros((P, NCON), np.float32)

    def put(name, a):
        out[:, CON[name]:CON[name] + a.shape[1]] = a

    put("ident", (i == j) * 1.0)
    put("ones", np.ones((P, P)))
    put("mean1024", np.full((P, P), 1.0 / 1024))
    put("mean256", np.full((P, P), 1.0 / 256))
    put("mean128", np.full((P, P), 1.0 / 128))
    put("upto", (i <= j) * 1.0)
    put("before", (i < j) * 1.0)
    put("from_", (i >= j) * 1.0)
    rot = np.zeros((P, P))
    for d in range(P):
        if d % 32 < 16:
            rot[d + 16, d] = -1.0
        else:
            rot[d - 16, d] = 1.0
    put("rot", rot)
    t = np.arange(T)
    inv = (np.float32(10000.0) ** (-np.arange(16, dtype=np.float32) / np.float32(16))).astype(np.float32)
    d = np.arange(P) % 64
    place = np.where((d < 32)[:, None], (t // 64)[None, :], (t % 64)[None, :]).astype(np.float32)
    angle = (place * inv[d % 16][:, None]).astype(np.float32)
    put("cos", np.cos(angle))
    put("sin", np.sin(angle))
    put("slot", np.broadcast_to(np.arange(CAP), (P, CAP)))
    parts = []
    for qt, keys in ((1, 256), (0, 128)):
        for steps, dil in ((128, 1), (128, 4), (128, 16)):
            dist = (qt * P + np.arange(P))[:, None] - np.arange(keys)[None, :]
            ok = (dist >= 0) & (dist % dil == 0) & (dist <= steps * dil)
            parts.append(np.where(ok, 0.0, NEG))
    put("mask", np.concatenate(parts, 1))
    put("lower", np.where(j <= i, 0.0, NEG))
    put("upper", np.where(j >= i, 0.0, NEG))
    return out


class Steps:

    def __init__(self, eng, sem):
        self.eng, self.sem, self.n, self.base = eng, sem, 0, 0

    def do(self, ins):
        self.n += 1
        ins.then_inc(self.sem, 1)
        return self.n

    def ended(self, upto=None):
        self.eng.wait_ge(self.sem, self.base + (self.n if upto is None else upto))

    def __call__(self, ins):
        self.do(ins)
        self.ended()


def build(nc, d_x, d_ctx, d_par, d_con, d_mmask, d_rows, d_gatew, d_routerw, d_b1, d_b2, d_dense, d_experts, d_out):
    ctx = ExitStack()
    with ctx:
        sems = {}

        norms = ["n0", "ln", "n1", "n2", "n3", "n4", "n6", "n7", "n8", "nc", "n9"]
        shared = {}
        for kind, count, stages in (
                ("sq", KT, norms + ["hm", "do", "n10", "n11"]), ("sum", 1, norms + ["n10", "n11"]),
                ("root", 1, norms + ["n10", "n11"]), ("x", KT, ["n1", "n3", "n6", "n8", "n11"]),
                ("h", KT, ["n0", "n2", "n4", "n5", "n7", "n11"]), ("h", KT, ["ln", "nc", "n9", "n10"]),
                ("p", KT, ["nc", "n9", "n10"]), ("tap", 2 * FT, ["ffn0", "ffn1"]), ("silu", FT, ["ffn0", "ffn1"]),
                ("act", FT, ["ffn0", "ffn1"]), ("out_slab", FT // 2, ["ffn0", "ffn1"])):
            for i, s in enumerate(stages):
                shared[f"{s}_{kind}"] = (f"{kind}_from_{stages[0]}_on", i * count)

        def before(name):
            return shared.get(name, (name, 0))[1]

        def sem(name):
            name = shared.get(name, (name, 0))[0]
            if name not in sems:
                sems[name] = ctx.enter_context(nc.semaphore(name))
            return sems[name]

        def sb(name, n, parts=P):
            return ctx.enter_context(nc.sbuf_tensor(name, [parts, n], F32))

        ring = sb("ring", RING * SLAB)
        X = sb("X", KT * T)[:, :].rearrange("p (c t) -> p c t", c=KT)
        par = sb("par", NPAR)
        con = sb("con", NCON)
        rows = sb("rows", NROW)
        arena_n = 29400
        arena = sb("arena", arena_n)
        small = sb("small", 512)
        banks = [ctx.enter_context(nc.psum_tensor(f"bank{i}", [P, 512], F32)) for i in range(8)]

        def C(name, n=128, at=0):
            return con[:, CON[name] + at:CON[name] + at + n]

        def par_col(name, i):
            return par[:, PAR[name] + i:PAR[name] + i + 1]

        def area(at, n):
            assert at + n <= arena_n, (at, n)
            return arena[:, at:at + n]

        def tiles(ap, c):
            return ap.rearrange("p (c t) -> p c t", c=c)

        ident, ones = C("ident"), C("ones")

        H = tiles(area(0, 2048), KT)
        SQ = tiles(area(2048, 2048), KT)
        RS = area(4096, 512)
        TMP = area(4608, 1024)
        NB = 5632
        PADW = TAPS - 1 + T
        G = tiles(area(NB, KT * PADW), KT)
        U = tiles(area(NB + 2304, 2048), KT)
        SG = tiles(area(NB + 15000, 2048), KT)
        DIAG = tiles(area(NB + 7000, 2 * TAPS * P), 2 * TAPS)
        Y = tiles(area(NB + 4864, 2048), KT)
        F_CA = tiles(area(NB, 512), 2)
        F_CG = tiles(area(NB + 512, 512), 2)
        F_SG = tiles(area(NB + 1024, 512), 2)
        F_ACT = tiles(area(NB + 1536, FT * T), FT)
        K_T = tiles(area(NB, 24 * T), 24)
        V_T = tiles(area(NB + 6144, 24 * T), 2)
        Q_T = tiles(area(NB + 12288, 24 * T), 24)
        MERGED = H
        A_S = [area(NB + 18432 + 1152 * i, 1152) for i in range(2)]
        A_P = [area(NB + 20736 + 1152 * i, 1152) for i in range(2)]
        A_PT = area(4096, 1152)
        A_SM = [area(NB + 23040 + 16 * i, 16) for i in range(2)]
        UC = tiles(area(NB, 2048), KT)
        MQ = tiles(area(NB + 2048, 1024), 4)
        MK = tiles(area(NB + 3072, 2048), 4)
        MV = tiles(area(NB + 5120, 4096), 4)
        HM = tiles(area(NB + 9216, 2048), KT)
        DQ = tiles(area(NB + 11264, 2048), KT)
        DK = tiles(area(NB + 13312, 4096), KT)
        DV = tiles(area(NB + 17408, 4096), 4)
        DO = tiles(area(NB + 21504, 2048), KT)
        CT = DO
        MMASK = tiles(area(2048, 2048), 4)
        GT = tiles(TMP[:, 0:64], 4)
        LF, BT, RR = (tiles(TMP[:, 64 + 32 * i:96 + 32 * i], 4) for i in range(3))
        AB = tiles(TMP[:, 160:192], 4)
        MX, NM, BM, EXM, DEN, REC = (TMP[:, 192 + 4 * i:196 + 4 * i] for i in range(6))
        RT = TMP[0:8, 512:1024]
        ME = tiles(area(NB, 2048), 4)
        MP = tiles(area(NB + 21504, 1024), 2)
        MPT = tiles(area(NB + 22528, 1024), 4)
        DP = [tiles(area(NB + 2048 + 2048 * i, 2048), 4) for i in range(2)]
        DPT = tiles(area(NB, 1024), 4)
        GO, GA, GB = (tiles(area(NB + 2048 * i, 2048), KT) for i in (1, 2, 3))
        YM = tiles(area(NB + 11264, 2048), KT)
        RSM = area(NB + 13312, 1024)
        RSD = area(NB + 14336, 2048)
        SQD = tiles(area(NB + 17408, 2048), KT)
        U2T = tiles(area(NB, 2048), 2)
        YACC = tiles(area(NB + 2048, 2048), KT)
        XGT = tiles(area(NB + 4096, 1024), KT)
        GL, LN, SGM = (tiles(area(NB + 5120 + 512 * i, 512), 2) for i in range(3))
        ACTT = tiles(area(NB + 6656, 1024), 8)
        YE = area(NB + 7680, 1024)
        SGT = area(NB + 8704, 256)
        SEL = tiles(area(NB + 8960, 256), 2)
        SELG = tiles(area(NB + 9216, 256), 2)
        NCOL = 4 * EXPERTS + 2
        POSA = tiles(area(NB + 9472, 2 * NCOL), 2)
        GATA = tiles(area(NB + 9472 + 2 * NCOL, 2 * NCOL), 2)
        MO = NB + 9472 + 4 * NCOL
        POSC = tiles(area(MO + 32, 8), 2)
        GATC = tiles(area(MO + 40, 4), 2)
        NEXT = arena[:, MO + 44:MO + 45].bitcast(I32)
        SR = [area(MO + 64 + 64 * i, 64) for i in range(9)]
        GTT = arena[0:EXPERTS, MO + 640:MO + 896]
        MORE = [area(NB + 11264 + SLAB * i, SLAB) for i in range(EXPERT_RING - RING)]
        B2 = arena[0:EXPERTS, NB + 19456:NB + 20480]
        ACTS = tiles(area(NB + 19456, 1024), 4)
        B1 = arena[0:EXPERTS, NB + 21504:NB + 23552]
        ONEH = arena[0:EXPERTS, MO + 896:MO + 1024]
        MOD = tiles(small[:, 0:96], 48)
        CS = tiles(small[:, 96:112], 8)
        EPS_COL = small[:, 120:121]
        ONE_COL = small[:, 122:123]
        GS1 = tiles(small[:, 128:144], 8)
        GS2 = small[:, 144:152]
        LAM = small[:, 152:160]
        LW = small[:, 160:288]
        DMX, DNM, DDEN, DREC = ([small[:, 288 + 8 * i + 4 * b:292 + 8 * i + 4 * b] for b in range(2)] for i in range(4))
        GW = small[:, 320:448].rearrange("p (k n) -> p k n", k=KT)
        RW = area(NB + 20480, 256).rearrange("p (k n) -> p k n", k=KT)

        def slab(g):
            return ring[:, (g % RING) * SLAB:(g % RING + 1) * SLAB]

        def expert_slab(j):
            q = j % EXPERT_RING
            return slab(DENSE_SLABS + q) if q < RING else MORE[q - RING]

        def slot_sem(j):
            q = j % EXPERT_RING
            return sem(f"slab{(DENSE_SLABS + q) % RING if q < RING else q}")

        def slab_loaded(eng, g):
            eng.wait_ge(sem(f"slab{g % RING}"), 16 * (g // RING + 1))

        def unit_ready(eng, u):
            eng.wait_ge(sem(f"unit{u % UNIT_BANKS}"), u // UNIT_BANKS + 1)

        def unit_half(eng, u, halves):
            eng.wait_ge(sem(f"read{u % UNIT_BANKS}"), 2 * (u // UNIT_BANKS) + halves)

        def read_sem(u):
            return sem(f"read{u % UNIT_BANKS}")

        def ubank(u):
            return banks[u % UNIT_BANKS]

        loaded = {}

        def units_read(eng, name):
            last = FIRST_UNIT[name] + UNITS_OF[name]
            for u in range(last - UNIT_BANKS, last):
                unit_half(eng, u, 2)

        def half_of(u, j):
            return ubank(u)[:, j * T:(j + 1) * T]

        stage_of = []
        for name, k, w in SCHEDULE:
            stage_of += [(name, i) for i in range(k)]

        def slab_used(eng, g):
            name, i = stage_of[g]
            if UNITS_OF[name]:
                unit_ready(eng, FIRST_UNIT[name] + ((i + 1) * UNITS_OF[name] - 1) // SLABS_OF[name])
            else:
                eng.wait_ge(sem(name + "_slab"), before(name + "_slab") + i + 1)

        def extra_passes(eng):
            eng.wait_ge(sem("extra"), 1)
            return eng.value_load(NEXT[0:1, 0:1], min_val=0, max_val=3)

        def passes(eng, body, first=None):
            with eng.Fori(0 if first is None else first, PAIRS) as p:
                body(p)
            extra = extra_passes(eng)
            loaded[eng] = extra
            with eng.If(extra > 0):
                with eng.Fori(PAIRS, (extra + 1) * PAIRS) as n:
                    body(n)

        def total_pairs(eng):
            return (loaded[eng] + 1) * PAIRS

        second = []
        for i in range(2):
            second.append((FIRST_UNIT["mq"] + i, [MQ[:, 2 * i + j, :] for j in range(2)]))
        for name, to in (("mk", MK), ("mv", MV), ("dq", DQ), ("dk", DK), ("dv", DV)):
            for i in range(SLABS_OF[name]):
                if name == "dq":
                    second.append((FIRST_UNIT[name] + i, [to[:, 2 * i + j, :] for j in range(2)]))
                    continue
                for half in range(2):
                    if name in ("mk", "dk"):
                        dst = [to[:, 2 * i + j, half * T:(half + 1) * T] for j in range(2)]
                    else:
                        dst = [to[:, 2 * half + j, i * T:(i + 1) * T] for j in range(2)]
                    second.append((FIRST_UNIT[name] + 2 * i + half, dst))

        def kvq(i, j):
            if i < 12:
                return K_T[:, 2 * i + j, :]
            return V_T[:, j, (i - 12) * T:(i - 11) * T] if i < 24 else Q_T[:, 2 * (i - 24) + j, :]

        def acc(c):
            return banks[WORK + c // 2][:, (c % 2) * T:(c % 2 + 1) * T]

        block = ctx.enter_context(nc.Block())

        @block.sync
        def _(sp):
            sp.dma_start(X, d_x).then_inc(sem("x_in"), 16)
            first = CON["upto"]
            sp.dma_start(con[:, 0:first], d_con[:, 0:first]).then_inc(sem("con_in"), 16)
            sp.dma_start(par[:, :], d_par).then_inc(sem("par_in"), 16)
            for g in range(DENSE_SLABS):
                if g == 2:
                    sp.dma_start(con[:, first:NCON], d_con[:, first:NCON]).then_inc(sem("tables_in"), 16)
                    sp.dma_start(rows[:, :], d_rows).then_inc(sem("rows_in"), 16)
                    sp.dma_start(GW, d_gatew).then_inc(sem("gatew_in"), 16)
                if g == FIRST_SLAB["mq"] + 1:
                    sp.wait_ge(sem("ffn1_out_slab"), before("ffn1_out_slab") + 11)
                    sp.dma_start(CT, d_ctx).then_inc(sem("ctx_in"), 16)
                if g == FIRST_SLAB["dk"]:
                    sp.wait_ge(sem("n9_sum"), before("n9_sum") + 1)
                    sp.dma_start(MMASK, tiles(d_mmask, 4)).then_inc(sem("mmask_in"), 16)
                if g == FIRST_SLAB["wa"]:
                    sp.wait_ge(sem("d_pv"), HEADS)
                    sp.dma_start(RW, d_routerw).then_inc(sem("routerw_in"), 16)
                    sp.dma_start(B2, d_b2).then_inc(sem("b2_in"), 16)
                if g >= RING:
                    slab_used(sp, g - RING)
                sp.dma_start(slab(g), d_dense[g]).then_inc(sem(f"slab{g % RING}"), 16)
            def expert_used(n, j):
                if j < 16:
                    sp.wait_ge(sem("up"), n * 8 + (j // 2 + 1))
                else:
                    sp.wait_ge(sem("down"), n * 4 + (4 + (j - 16) // 2 + 1))

            for j in range(24):
                if j < RING:
                    slab_used(sp, DENSE_SLABS + j - RING)
                elif j < EXPERT_RING:
                    unit_ready(sp, FIRST_UNIT["wo"] + 3)
                else:
                    expert_used(0, j - EXPERT_RING)
                sp.dma_start(expert_slab(j), d_experts[j]).then_inc(slot_sem(j), 16)
                if j == RING:
                    sp.dma_start(B1, d_b1).then_inc(sem("b1_in"), 16)

            def body(n):
                p = n % PAIRS
                for j in range(24):
                    if j < EXPERT_RING:
                        expert_used(n - 1, j + 24 - EXPERT_RING)
                    else:
                        expert_used(n, j - EXPERT_RING)
                    src = d_experts[bass.ds(p * 24 + j, 1)].rearrange("o p n -> (o p) n")
                    sp.dma_start(expert_slab(j), src).then_inc(slot_sem(j), 16)

            passes(sp, body, 1)
            sp.wait_ge(sem("n11_h"), before("n11_h") + KT)
            sp.dma_start(d_out, H).then_inc(sem("out_done"), 16)
            sp.wait_ge(sem("out_done"), 16)

        @block.tensor
        def _(pe):
            def product(u, g, src, token_major=False, wait_chunk=None):
                w = slab(g).rearrange("p (k n) -> p k n", k=KT)
                slab_loaded(pe, g)
                if u >= UNIT_BANKS:
                    unit_half(pe, u - UNIT_BANKS, 2)
                for j in range(2):
                    for k in range(KT):
                        if wait_chunk and j == 0:
                            wait_chunk(k)
                        o = ubank(u)[:, j * T:(j + 1) * T]
                        if token_major:
                            ins = nc.tensor.matmul(o, src[:, k, j * P:(j + 1) * P], w[:, k, :],
                                                   start=(k == 0), stop=(k == KT - 1))
                        else:
                            ins = nc.tensor.matmul(o, w[:, k, j * P:(j + 1) * P], src[:, k, :],
                                                   start=(k == 0), stop=(k == KT - 1))
                ins.then_inc(sem(f"unit{u % UNIT_BANKS}"), 1)

            def stage(name, src, ready=None, token_major=False, first=0, count=None):
                n = SLABS_OF[name] if count is None else count
                for i in range(first, first + n):
                    wait = (lambda k: pe.wait_ge(sem(ready), before(ready) + k + 1)) if ready and i == first else None
                    product(FIRST_UNIT[name] + i, FIRST_SLAB[name] + i, src, token_major, wait)

            def stat(name, half, mat, sq=SQ):
                for c in range(KT):
                    pe.wait_ge(sem(name + "_sq"), before(name + "_sq") + c + 1)
                    ins = nc.tensor.matmul(banks[STAT][:, half * T:(half + 1) * T], mat, sq[:, c, :],
                                           start=(c == 0), stop=(c == KT - 1))
                ins.then_inc(sem(name + "_sum"), 1)

            def ada(name, first=0, end=None):
                for i in range(first, SLABS_OF[name] if end is None else end):
                    g, u = FIRST_SLAB[name] + i, FIRST_UNIT[name] + i // 2
                    w = slab(g).rearrange("p (k n) -> p k n", k=KT)
                    slab_loaded(pe, g)
                    if i == 0:
                        pe.wait_ge(sem("silu_c"), 2)
                    if i % 2 == 0 and u >= UNIT_BANKS:
                        unit_half(pe, u - UNIT_BANKS, 2)
                    for j in range(2):
                        m = 2 * (i % 2) + j
                        for k in range(KT):
                            ins = nc.tensor.matmul(ubank(u)[:, 64 * m:64 * m + 64].rearrange("p (v n) -> p v n", v=2),
                                                   w[:, k, j * P:(j + 1) * P],
                                                   CS[:, k, :].unsqueeze(2).to_broadcast([P, 2, 32]),
                                                   start=(k == 0), stop=(k == KT - 1))
                    if i % 2:
                        ins.then_inc(sem(f"unit{u % UNIT_BANKS}"), 1)

            def ffn_out(layer):
                name = f"ffn{layer}_out"
                for i in range(SLABS_OF[name]):
                    g = FIRST_SLAB[name] + i
                    w = slab(g).rearrange("p (k n) -> p k n", k=2)
                    slab_loaded(pe, g)
                    for kk in range(2):
                        k = 2 * i + kk
                        pe.wait_ge(sem(f"ffn{layer}_act"), before(f"ffn{layer}_act") + k + 1)
                        for m in range(KT):
                            ins = nc.tensor.matmul(
                                banks[WORK + m // 2][:, (m % 2) * T:(m % 2 + 1) * T],
                                w[:, kk, m * P:(m + 1) * P], F_ACT[:, k, :],
                                start=(k == 0 and m % 2 == 0), stop=(k == FT - 1), skip_group_check=True)
                    ins.then_inc(sem(name + "_slab"), 1)

            def attention():
                def scores(h):
                    if h:
                        pe.wait_ge(sem("att_masked"), 4 * h)
                    for qt, keys, ats in ((1, 256, (0, 256, 512)), (0, 128, (768, 896, 1024))):
                        for g in range(GROUPS):
                            at = ats[g]
                            ins = nc.tensor.matmul(
                                banks[WORK + at // 512][:, at % 512:at % 512 + keys],
                                Q_T[:, g * HEADS + h, qt * P:(qt + 1) * P], K_T[:, g * HEADS + h, 0:keys],
                                start=True, stop=True)
                    ins.then_inc(sem("att_scores"), 1)

                pe.wait_ge(sem("tables_in"), 16)
                units_read(pe, "q")
                units_read(pe, "ada4") if UNITS_OF["ada4"] >= UNIT_BANKS else unit_half(pe, FIRST_UNIT["ada4"], 2)
                scores(0)
                for h in range(HEADS):
                    if h + 1 < HEADS:
                        scores(h + 1)
                    for n in range(9):
                        if n == 0:
                            pe.wait_ge(sem("att_p"), 2 * h + 1)
                        if n == 6:
                            pe.wait_ge(sem("att_p"), 2 * h + 2)
                        if h and n % 4 == 0:
                            pe.wait_ge(sem("att_pt"), 3 * (h - 1) + n // 4 + 1)
                        ins = nc.tensor.transpose(banks[n // 4][:, (n % 4) * P:(n % 4 + 1) * P],
                                                  A_P[h % 2][:, n * P:(n + 1) * P], ident)
                        if n in (3, 7, 8):
                            ins.then_inc(sem("att_tr"), 1)
                    pe.wait_ge(sem("att_pt"), 3 * h + 3)
                    if h:
                        pe.wait_ge(sem("att_out"), h)
                    o = banks[7][:, 0:T]
                    for g in range(GROUPS):
                        v = V_T[:, 0, (g * HEADS + h) * P:(g * HEADS + h + 1) * P]
                        nc.tensor.matmul(o[:, 0:P], v, A_PT[:, (6 + g) * P:(7 + g) * P],
                                         start=(g == 0), stop=(g == 2), skip_group_check=True)
                    for g in range(GROUPS):
                        for kt in range(2):
                            v = V_T[:, kt, (g * HEADS + h) * P:(g * HEADS + h + 1) * P]
                            ins = nc.tensor.matmul(o[:, P:T], v, A_PT[:, (2 * g + kt) * P:(2 * g + kt + 1) * P],
                                                   start=(g == 0 and kt == 0), stop=(g == 2 and kt == 1),
                                                   skip_group_check=True)
                    ins.then_inc(sem("att_pv"), 1)

            mean = C("mean1024")
            pe.wait_ge(sem("con_in"), 16)
            stat("n0", 0, mean)
            ada("ada0")
            stage("cm_in", H, "n0_h")
            ada("ada1")
            for c in (6, 7):
                pe.wait_ge(sem("glu"), c + 1)
                for k in range(TAPS):
                    n = (c - 6) * TAPS + k
                    pe.wait_ge(sem("diag"), n + 1)
                    ins = nc.tensor.matmul(banks[WORK + 1][:, (c - 6) * T:(c - 5) * T], DIAG[:, n, :], G[:, c, k:k + T],
                                           start=(k == 0), stop=(k == TAPS - 1))
            ins.then_inc(sem("conv_pe"), 1)
            for c in range(KT):
                pe.wait_ge(sem("conv"), c + 1)
                ins = nc.tensor.matmul(banks[WORK][:, 0:T], mean, U[:, c, :], start=(c == 0), stop=(c == KT - 1))
            ins.then_inc(sem("ln_mean"), 1)
            stat("ln", 1, mean)
            stage("cm_out", H, "ln_h")
            stat("n1", 0, mean)
            ada("ada2")
            stat("n2", 1, mean)
            stage("ffn0_in", H, "n2_h")
            ffn_out(0)
            stat("n3", 0, mean)
            ada("ada3")
            stat("n4", 1, mean)
            stage("kv", H, "n4_h", count=12)
            stage("kv", H, token_major=True, first=12, count=12)
            stage("q", SQ, "n5_h")
            ada("ada4")
            attention()
            stage("o", MERGED, "att_out")
            stat("n6", 0, mean)
            ada("ada5")
            stat("n7", 1, mean)
            stage("ffn1_in", H, "n7_h")
            ffn_out(1)
            stat("n8", 0, mean)
            stat("nc", 1, mean)
            pe.wait_ge(sem("nc_root"), before("nc_root") + 1)
            stat("n9", 0, mean)

            def two(name, token_major=False):
                for i in range(SLABS_OF[name]):
                    for half, (src, h) in enumerate(((UC, "nc_h"), (H, "n9_h"))):
                        pe.wait_ge(sem(h), before(h) + KT)
                        product(FIRST_UNIT[name] + 2 * i + half, FIRST_SLAB[name] + i, src, token_major)

            stage("mq", H, "n9_h")
            pe.wait_ge(sem("nc_h"), before("nc_h") + KT)
            pe.wait_ge(sem("n8_x"), before("n8_x") + KT)
            pe.wait_ge(sem("gatew_in"), 16)
            for t in range(4):
                src = (UC, H)[t // 2]
                for k in range(KT):
                    ins = nc.tensor.matmul(banks[4][:, 16 * t:16 * t + 16], src[:, k, (t % 2) * P:(t % 2 + 1) * P],
                                           GW[:, k, :], start=(k == 0), stop=(k == KT - 1))
            ins.then_inc(sem("gates"), 1)
            two("mk")
            pe.wait_ge(sem("logf"), 1)
            for d, (tri, order) in enumerate(((C("upto"), (0, 1, 2, 3)), (C("from_"), (1, 0, 3, 2)))):
                for n, t in enumerate(order):
                    o = banks[5][:, 8 * t + 4 * d:8 * t + 4 * d + 4]
                    for i in range(n + 1):
                        ins = nc.tensor.matmul(o, tri if i == n else ones, LF[:, order[i], 4 * d:4 * d + 4],
                                               start=(i == 0), stop=(i == n))
            ins.then_inc(sem("cumf"), 1)
            two("mv", True)
            pe.wait_ge(sem("rr"), 1)
            for t in range(4):
                ins = nc.tensor.transpose(banks[6][0:8, t * P:(t + 1) * P], RR[:, t, :], ident)
            ins.then_inc(sem("rr_t"), 1)
            stage("dq", H)
            two("dk")
            units_read(pe, "dk")
            pe.wait_ge(sem("rt"), 1)

            def turned(r, c):
                if r:
                    pe.wait_ge(sem("rope"), c + 2)
                for t in (c, c + 1):
                    ins = nc.tensor.matmul(acc(t), C("rot"), DQ[:, t, :] if r == 0 else DK[:, t, T:], start=True, stop=True)
                ins.then_inc(sem("turned"), 1)

            for c in range(0, KT, 2):
                turned(0, c)
            for i in range(8):
                product(FIRST_UNIT["dv"] + i, FIRST_SLAB["dv"] + i // 2, (UC, H)[i % 2], True)
                if 2 <= i < 6:
                    turned(1, 2 * (i - 2))

            units_read(pe, "dv")
            for h in range(4):
                if h == 0:
                    pe.wait_ge(sem("rope"), 16)
                else:
                    pe.wait_ge(sem("m_pt"), 2 * h)
                    pe.wait_ge(sem("m_out"), h)
                for qt in range(2):
                    nc.tensor.matmul(banks[4 + qt][:, :], MQ[:, h, qt * P:(qt + 1) * P], MK[:, h, :],
                                     start=True, stop=True)
                for d in range(2):
                    pick = ident[0:8, 4 * d + h:4 * d + h + 1].to_broadcast([8, P])
                    ins = nc.tensor.matmul(banks[6 + d][:, :], pick, RT, start=True, stop=True)
                ins.then_inc(sem("m_scores"), 1)
                ada("ada6", *{0: (0, 4), 1: (4, 8), 2: (8, 10), 3: (10, 12)}[h])
                pe.wait_ge(sem("m_p"), 2 * h + 2)
                for kt in range(4):
                    for qt in range(2):
                        ins = nc.tensor.transpose(banks[6 + kt // 2][:, (kt % 2) * T + qt * P:(kt % 2) * T + (qt + 1) * P],
                                                  MP[:, qt, kt * P:(kt + 1) * P], ident)
                    if kt % 2:
                        ins.then_inc(sem("m_tr"), 1)
                pe.wait_ge(sem("m_pt"), 2 * h + 2)
                for v in range(2):
                    for kt in range(4):
                        at = h * T + v * P
                        ins = nc.tensor.matmul(banks[4][:, v * T:(v + 1) * T], MV[:, kt, at:at + P], MPT[:, kt, :],
                                               start=(kt == 0), stop=(kt == 3))
                ins.then_inc(sem("m_pv"), 1)

            def d_scores(h):
                if h == 0:
                    pe.wait_ge(sem("m_pt"), 8)
                    pe.wait_ge(sem("m_out"), 4)
                else:
                    pe.wait_ge(sem("d_exp"), 4 * h)
                for m in range(2):
                    for qt in range(2):
                        ins = nc.tensor.matmul(banks[4 + 2 * m + qt][:, :], DQ[64 * m:64 * m + 64, h, qt * P:(qt + 1) * P],
                                               DK[64 * m:64 * m + 64, h, :], start=True, stop=True)
                        ins.then_inc(sem("d_scores"), 1)

            d_scores(0)
            units_read(pe, "ada6")
            for h in range(HEADS):
                if h + 1 < HEADS:
                    d_scores(h + 1)
                for kt in range(4):
                    for qt in range(2):
                        if kt == 0:
                            pe.wait_ge(sem("d_a"), 2 * h + qt + 1)
                        if qt == 0 and kt % 2 == 0 and h:
                            pe.wait_ge(sem("d_pt"), 2 * (h - 1) + kt // 2 + 1)
                        ins = nc.tensor.transpose(banks[kt // 2][:, (kt % 2) * T + qt * P:(kt % 2) * T + (qt + 1) * P],
                                                  DP[h % 2][:, qt, kt * P:(kt + 1) * P], ident)
                    if kt % 2:
                        ins.then_inc(sem("d_tr"), 1)
                pe.wait_ge(sem("d_pt"), 2 * h + 2)
                if h:
                    pe.wait_ge(sem("d_out"), h)
                for kt in range(4):
                    ins = nc.tensor.matmul(banks[2][:, 0:T], DV[:, kt, h * P:(h + 1) * P], DPT[:, kt, :],
                                           start=(kt == 0), stop=(kt == 3))
                ins.then_inc(sem("d_pv"), 1)
            pe.wait_ge(sem("d_out"), HEADS)
            stage("go", H)
            for h in range(4):
                for v in range(2):
                    pe.wait_ge(sem("hm_sq"), 2 * h + v + 1)
                    ins = nc.tensor.matmul(banks[4 + h // 2][:, (h % 2) * T:(h % 2 + 1) * T], C("mean256"), SQ[:, 2 * h + v, :],
                                           start=(v == 0), stop=(v == 1))
            ins.then_inc(sem("hm_sum"), 1)
            stage("ga", H)
            pe.wait_ge(sem("hm_root"), 2)
            for h in range(HEADS):
                pe.wait_ge(sem("do_sq"), h + 1)
                ins = nc.tensor.matmul(acc(h), C("mean128"), SQD[:, h, :], start=True, stop=True)
            ins.then_inc(sem("do_sum"), 1)
            stage("gb", H)
            stage("wa", HM, "a_out")
            stage("wb", DO, "b_out")
            stage("wo", YM, "ym")
            stat("n10", 1, mean)
            pe.wait_ge(sem("do_root"), 4)
            for t in range(2):
                for c in range(KT):
                    if t == 0:
                        pe.wait_ge(sem("n10_h"), before("n10_h") + c + 1)
                    ins = nc.tensor.transpose(banks[4 + 2 * t + c // 4][:, (c % 4) * P:(c % 4 + 1) * P],
                                              H[:, c, t * P:(t + 1) * P], ident)
                    if c % 4 == 3:
                        ins.then_inc(sem("u2_tr"), 1)
            units_read(pe, "wo")
            pe.wait_ge(sem("routerw_in"), 16)
            for t in range(2):
                for k in range(KT):
                    ins = nc.tensor.matmul(banks[0][:, 32 * t:32 * t + 32], H[:, k, t * P:(t + 1) * P], RW[:, k, :],
                                           start=(k == 0), stop=(k == KT - 1))
            ins.then_inc(sem("logits"), 1)
            pe.wait_ge(sem("chosen"), 2)
            M0, M1 = SR[0][:, 0:32], SR[0][:, 32:64]
            nc.tensor.matmul(banks[1][:, 0:32], C("before"), M0, start=True, stop=True)
            nc.tensor.matmul(banks[1][:, 32:64], ones, M0, start=True, stop=False)
            nc.tensor.matmul(banks[1][:, 32:64], C("before"), M1, start=False, stop=True)
            nc.tensor.matmul(banks[1][:, 64:96], ones, M0, start=True, stop=False)
            nc.tensor.matmul(banks[1][:, 64:96], ones, M1, start=False, stop=True).then_inc(sem("places"), 1)
            pe.wait_ge(sem("gate_w"), 2)
            for t in range(2):
                ins = nc.tensor.transpose(banks[2][0:EXPERTS, t * P:(t + 1) * P], SR[1][:, 32 * t:32 * t + 32], ident)
            ins.then_inc(sem("gate_t"), 1)
            pe.wait_ge(sem("gtt"), 1)
            pe.wait_ge(sem("b2_in"), 16)
            pe.wait_ge(sem("u2_out"), 4)
            for c in range(KT):
                ins = nc.tensor.matmul(acc(c), B2[:, c * P:(c + 1) * P], GTT, start=True, stop=True)
                if c % 2:
                    ins.then_inc(sem("b2_done"), 1)

            def gather(n):
                pe.wait_ge(sem("sel"), n + 1)
                for b in range(2):
                    for c in range(4 * b, 4 * b + 4):
                        for t in range(2):
                            ins = nc.tensor.matmul(banks[4 + b][:, (c % 4) * P:(c % 4 + 1) * P], U2T[:, t, c * P:(c + 1) * P],
                                                   SEL[:, t, :], start=(t == 0), stop=(t == 1))
                    ins.then_inc(sem("gathered"), 1)

            def scatter(n):
                pe.wait_ge(sem("ye"), n * 2 + 1)
                pe.wait_ge(sem("sgt"), n + 1)
                for j in range(4):
                    pe.wait_ge(sem("scat_read"), n * 4 + (j + 1))
                    for c in (2 * j, 2 * j + 1):
                        ins = nc.tensor.matmul(banks[6 + j % 2][:, (c % 2) * T:(c % 2 + 1) * T], YE[:, c * P:(c + 1) * P],
                                               SGT, start=True, stop=True)
                    ins.then_inc(sem("scattered"), 1)

            def expert_loaded(n, j):
                q = j % EXPERT_RING
                earlier = (DENSE_SLABS + q) // RING if q < RING else 0
                pe.wait_ge(slot_sem(j), n * (16 * 24 // EXPERT_RING) + 16 * (earlier + j // EXPERT_RING + 1))

            def up(n, first, end):
                for i in range(first, end):
                    if i % 2 == 0:
                        pe.wait_ge(sem("up_read"), n * 8 + (i + 2))
                    for e in range(2):
                        o = banks[i // 2 % 2][e * CAP:(e + 1) * CAP, i % 2 * T:(i % 2 + 1) * T]
                        nc.tensor.matmul(o, ONEH[:, e * CAP:(e + 1) * CAP], B1[:, i * T:(i + 1) * T], start=True, stop=False)
                        expert_loaded(n, 2 * i + e)
                    for k in range(KT):
                        for e in range(2):
                            o = banks[i // 2 % 2][e * CAP:(e + 1) * CAP, i % 2 * T:(i % 2 + 1) * T]
                            w = expert_slab(2 * i + e).rearrange("p (k n) -> p k n", k=KT)
                            ins = nc.tensor.matmul(o, XGT[:, k, e * CAP:(e + 1) * CAP], w[:, k, :],
                                                   start=False, stop=(k == KT - 1))
                    ins.then_inc(sem("up"), 1)

            def hidden(n):
                for c in range(4):
                    pe.wait_ge(sem("act"), n * 4 + (c + 3))
                    for j in range(2):
                        ins = nc.tensor.transpose(banks[6 + c // 2][:, (c % 2 * 2 + j) * P:(c % 2 * 2 + j + 1) * P],
                                                  ACTS[:, c, j * P:(j + 1) * P], ident)
                    if c % 2:
                        ins.then_inc(sem("act_t"), 1)

            def down(n):
                pe.wait_ge(sem("ye"), n * 2 + 1)
                for i in range(4):
                    for e in range(2):
                        expert_loaded(n, 16 + 2 * i + e)
                    if i % 2 == 0:
                        pe.wait_ge(sem("act_out"), n * 2 + (i // 2 + 1))
                    for kk in range(2):
                        k = 2 * i + kk
                        for half in range(2):
                            for e in range(2):
                                w = expert_slab(16 + 2 * i + e).rearrange("p (k n) -> p k n", k=2)
                                ins = nc.tensor.matmul(banks[2 + half][e * CAP:(e + 1) * CAP, :],
                                                       ACTT[:, k, e * CAP:(e + 1) * CAP],
                                                       w[:, kk, half * 512:(half + 1) * 512], start=(k == 0), stop=(k == 7))
                    ins.then_inc(sem("down"), 1)

            def body(n):
                pe.wait_ge(sem("hot"), n * 2 + 2)
                pe.wait_ge(sem("xgt"), n * 2 + 2)
                up(n, 0, 4)
                scatter(n)
                pe.wait_ge(sem("selg"), n + 1)
                for t in range(2):
                    ins = nc.tensor.transpose(banks[4][:, t * P:(t + 1) * P], SELG[:, t, :], ident)
                ins.then_inc(sem("selg_t"), 1)
                up(n, 4, 8)
                pe.wait_ge(sem("sgt"), n + 2)
                gather(n + 1)
                pe.wait_ge(sem("scat_read"), n * 4 + 6)
                hidden(n)
                down(n)

            pe.sem_inc(sem("down"), 4)
            pe.sem_inc(sem("act_t"), 2)
            pe.wait_ge(sem("b1_in"), 16)
            pe.sem_inc(sem("selg_t"), 1)
            pe.wait_ge(sem("b2_read"), 4)
            gather(0)
            passes(pe, body)
            n_end = total_pairs(pe)
            scatter(n_end)
            pe.wait_ge(sem("scat_read"), n_end * 4 + 6)
            stat("n11", 0, mean)

        @block.scalar
        def _(act):
            def square(name, src, ready=None, sq=SQ):
                for c in range(KT):
                    if ready:
                        act.wait_ge(sem(ready), before(ready) + c + 1)
                    nc.scalar.activation(sq[:, c, :], src(c), ACT.Square).then_inc(sem(name + "_sq"), 1)

            def root(name, half):
                if before(name + "_root"):
                    act.wait_ge(sem(name + "_root"), before(name + "_root"))
                nc.scalar.activation(small[:, 121:122], EPS_COL, ACT.Sqrt)
                act.wait_ge(sem(name + "_sum"), before(name + "_sum") + 1)
                nc.scalar.activation(RS[:, half * T:(half + 1) * T], banks[STAT][:, half * T:(half + 1) * T],
                                     ACT.Sqrt, bias=EPS_COL).then_inc(sem(name + "_root"), 1)

            def ada_copy(name, first=0, end=None):
                m = 2 * sum(k for n, k, _ in SCHEDULE if n.startswith("ada") and n < name)
                for i in range(first, UNITS_OF[name] if end is None else end):
                    u = FIRST_UNIT[name] + i
                    unit_ready(act, u)
                    src = tiles(ubank(u)[:, 0:256], 4)
                    for v in range(2):
                        nc.scalar.activation(MOD[:, m + 4 * i:m + 4 * i + 4, v], src[:, :, 32 * v],
                                             ACT.Copy).then_inc(read_sem(u), 1)

            def ffn_in(layer):
                name = f"ffn{layer}_in"
                for j in range(FT + 1):
                    if j < FT:
                        u = FIRST_UNIT[name] + j
                        unit_ready(act, u)
                        if j >= 2:
                            act.wait_ge(sem(f"ffn{layer}_act"), before(f"ffn{layer}_act") + j - 1)
                        for half, buf in ((0, F_CA), (1, F_CG)):
                            c = half * FT + j
                            nc.scalar.activation(buf[:, j % 2, :], half_of(u, half), ACT.Identity,
                                                 bias=par_col("ffn_dw_b", layer * 44 + c),
                                                 scale=par_col("ffn_dw", (layer * 3 + 2) * 44 + c))\
                              .then_inc(sem(f"ffn{layer}_tap"), 1)
                    if j >= 1:
                        unit_half(act, FIRST_UNIT[name] + j - 1, 2)
                        nc.scalar.activation(F_SG[:, (j - 1) % 2, :], F_CG[:, (j - 1) % 2, :],
                                             ACT.Silu).then_inc(sem(f"ffn{layer}_silu"), 1)

            def attention():
                def exps(h):
                    S, Pm, sm = A_S[h % 2], A_P[h % 2], A_SM[h % 2]
                    for i, (a, b) in enumerate(((0, 768), (768, 1152))):
                        act.wait_ge(sem("att_max"), 2 * h + i + 1)
                        if h >= 2 and i == 0:
                            act.wait_ge(sem("att_tr"), 3 * (h - 1))
                        nc.scalar.activation(Pm[:, a:b], S[:, a:b], ACT.Exp, bias=sm[:, 2 + i:3 + i],
                                             accum_out=sm[:, 4 + i:5 + i]).then_inc(sem("att_exp"), 1)

                exps(0)
                for h in range(HEADS):
                    for n in range(3):
                        act.wait_ge(sem("att_tr"), 3 * h + n + 1)
                        if h and n == 0:
                            act.wait_ge(sem("att_pv"), h)
                        w = 512 if n < 2 else 128
                        nc.scalar.copy(A_PT[:, n * 512:n * 512 + w], banks[n][:, 0:w])\
                          .then_inc(sem("att_pt"), 1)
                    if h + 1 < HEADS:
                        exps(h + 1)
                    act.wait_ge(sem("att_pv"), h + 1)
                    nc.scalar.copy(MERGED[:, h, :], banks[7][:, 0:T]).then_inc(sem("att_out"), 1)

            act.wait_ge(sem("eps_set"), 1)
            act.wait_ge(sem("x_in"), 16)
            square("n0", lambda c: X[:, c, :])
            root("n0", 0)
            act.wait_ge(sem("par_in"), 16)
            for i, name in enumerate(("c", "c_ctx")):
                nc.scalar.activation(CS[:, :, i], par[:, PAR[name]:PAR[name] + 8], ACT.Silu)\
                  .then_inc(sem("silu_c"), 1)
            ada_copy("ada0")
            for j in range(8):
                u = FIRST_UNIT["cm_in"] + j
                unit_ready(act, u)
                nc.scalar.activation(G[:, j, TAPS - 1:], half_of(u, 0), ACT.Identity,
                                     bias=par_col("cm_b_in", j)).then_inc(read_sem(u), 1)
                nc.scalar.activation(SG[:, j, :], half_of(u, 1), ACT.Sigmoid,
                                     bias=par_col("cm_b_in", 8 + j)).then_inc(read_sem(u), 1)
                for n in range(8 * j, min(8 * j + 8, 2 * TAPS)):
                    nc.scalar.activation(DIAG[:, n, :], ident, ACT.Copy,
                                         scale=par_col("cm_dw", n % TAPS * 8 + 6 + n // TAPS)).then_inc(sem("diag"), 1)
            ada_copy("ada1")
            square("ln", lambda c: U[:, c, :], "ln_centred")
            root("ln", 1)
            for c in range(KT):
                act.wait_ge(sem("ln_scaled"), c + 1)
                nc.scalar.activation(H[:, c, :], U[:, c, :], ACT.Silu, bias=par_col("cm_ln_b", c),
                                     scale=par_col("cm_ln_g", c)).then_inc(sem("ln_h"), 1)
            for j in range(8):
                u = FIRST_UNIT["cm_out"] + j // 2
                unit_ready(act, u)
                nc.scalar.activation(SQ[:, j, :], half_of(u, j % 2), ACT.Square,
                                     bias=par_col("cm_b_out", j)).then_inc(sem("n1_sq"), 1)
                nc.scalar.activation(Y[:, j, :], half_of(u, j % 2), ACT.Identity,
                                     bias=par_col("cm_b_out", j)).then_inc(read_sem(u), 1)
            root("n1", 0)
            ada_copy("ada2")
            square("n2", lambda c: X[:, c, :], "n1_x")
            root("n2", 1)
            ffn_in(0)
            act.wait_ge(sem("ffn0_out_slab"), before("ffn0_out_slab") + 11)
            square("n3", acc)
            root("n3", 0)
            ada_copy("ada3")
            square("n4", lambda c: X[:, c, :], "n3_x")
            root("n4", 1)
            for i in range(0, 36, 2):
                u = FIRST_UNIT["kv"] + i
                unit_ready(act, u)
                for j in range(2):
                    nc.scalar.copy(kvq(i, j), half_of(u, j)).then_inc(read_sem(u), 1)
            ada_copy("ada4")
            attention()
            for j in range(8):
                u = FIRST_UNIT["o"] + j // 2
                unit_ready(act, u)
                nc.scalar.activation(SQ[:, j, :], half_of(u, j % 2), ACT.Square).then_inc(sem("n6_sq"), 1)
                nc.scalar.copy(Y[:, j, :], half_of(u, j % 2)).then_inc(read_sem(u), 1)
            root("n6", 0)
            ada_copy("ada5")
            square("n7", lambda c: X[:, c, :], "n6_x")
            root("n7", 1)
            ffn_in(1)
            act.wait_ge(sem("ffn1_out_slab"), before("ffn1_out_slab") + 11)
            square("n8", acc)
            root("n8", 0)

            def shifted(name, v, m, dst):
                for c in range(KT):
                    act.wait_ge(sem(name + "_p"), before(name + "_p") + c + 1)
                    nc.scalar.activation(dst[:, c, :], dst[:, c, :], ACT.Identity, bias=MOD[:, m + c, v:v + 1])\
                      .then_inc(sem(name + "_h"), 1)

            def take(first, last):
                for i in range(first, last):
                    if i % 2 == 0:
                        u, dst = second[i]
                        unit_ready(act, u)
                        for j in range(2):
                            nc.scalar.copy(dst[j], half_of(u, j)).then_inc(read_sem(u), 1)

            act.wait_ge(sem("ctx_in"), 16)
            square("nc", lambda c: CT[:, c, :])
            root("nc", 1)
            square("n9", lambda c: X[:, c, :], "n8_x")
            root("n9", 0)
            shifted("nc", 1, 0, UC)
            shifted("n9", 0, 0, H)
            act.wait_ge(sem("lam_dot"), 1)
            nc.scalar.activation(LAM[:, 2:4], LAM[:, 0:2], ACT.Exp).then_inc(sem("lam_exp"), 1)
            take(0, 2)
            act.wait_ge(sem("abs_f"), 1)
            nc.scalar.activation(AB, AB, ACT.Exp, scale=-1.0).then_inc(sem("f_exp"), 1)
            act.wait_ge(sem("f_exp"), 1)
            nc.scalar.activation(AB, AB, ACT.Ln, bias=ONE_COL).then_inc(sem("f_ln"), 1)
            take(2, len(second))
            ada_n = 0
            for h in range(4):
                act.wait_ge(sem("m_nm"), h + 1)
                for i in range(4):
                    nc.scalar.activation(ME[:, i, :], ME[:, i, :], ACT.Exp, bias=NM[:, i:i + 1]).then_inc(sem("m_exp"), 1)
                nc.scalar.activation(EXM, BM, ACT.Exp).then_inc(sem("m_exp"), 1)
                k = (2, 2, 1, 1)[h]
                ada_copy("ada6", ada_n, ada_n + k)
                ada_n += k
                for b in range(2):
                    act.wait_ge(sem("m_tr"), 2 * h + b + 1)
                    nc.scalar.copy(MPT[:, 2 * b:2 * b + 2, :], tiles(banks[6 + b][:, :], 2)).then_inc(sem("m_pt"), 1)
                act.wait_ge(sem("m_pv"), h + 1)
                nc.scalar.copy(HM[:, 2 * h:2 * h + 2, :], tiles(banks[4][:, :], 2)).then_inc(sem("m_out"), 1)

            def d_exps(h):
                act.wait_ge(sem("d_nm"), h + 1)
                if h >= 2:
                    act.wait_ge(sem("d_tr"), 2 * (h - 1))
                for i in range(4):
                    nc.scalar.activation(DP[h % 2][:, i, :], banks[4 + i][:, :], ACT.Exp, bias=DNM[h % 2][:, i:i + 1],
                                         scale=SCALE_D, accum_out=DDEN[h % 2][:, i:i + 1]).then_inc(sem("d_exp"), 1)

            d_exps(0)
            for h in range(HEADS):
                for b in range(2):
                    act.wait_ge(sem("d_tr"), 2 * h + b + 1)
                    if h and b == 0:
                        act.wait_ge(sem("d_pv"), h)
                    nc.scalar.copy(DPT[:, 2 * b:2 * b + 2, :], tiles(banks[b][:, :], 2)).then_inc(sem("d_pt"), 1)
                if h + 1 < HEADS:
                    d_exps(h + 1)
                act.wait_ge(sem("d_pv"), h + 1)
                nc.scalar.copy(DO[:, h, :], banks[2][:, 0:T]).then_inc(sem("d_out"), 1)

            def gate(name, dst):
                for j in range(8):
                    u = FIRST_UNIT[name] + j // 2
                    unit_ready(act, u)
                    nc.scalar.activation(dst[:, j, :], half_of(u, j % 2), ACT.Sigmoid).then_inc(read_sem(u), 1)

            act.wait_ge(sem("m_out"), 4)
            act.wait_ge(sem("d_out"), HEADS)
            act.wait_ge(sem("d_pv"), HEADS)
            square("hm", lambda c: HM[:, c, :])
            square("do", lambda c: DO[:, c, :], sq=SQD)
            gate("go", GO)
            act.wait_ge(sem("hm_sum"), 1)
            for b in range(2):
                nc.scalar.activation(RSM[:, 512 * b:512 * b + 512], banks[4 + b][:, :], ACT.Sqrt, bias=EPS_COL)\
                  .then_inc(sem("hm_root"), 1)
            gate("ga", GA)
            act.wait_ge(sem("do_sum"), 1)
            for b in range(4):
                nc.scalar.activation(RSD[:, 512 * b:512 * b + 512], banks[4 + b][:, :], ACT.Sqrt, bias=EPS_COL)\
                  .then_inc(sem("do_root"), 1)
            gate("gb", GB)
            for c in range(KT):
                unit_half(act, FIRST_UNIT["wo"] + c // 2, c % 2 + 1)
                nc.scalar.activation(SQ[:, c, :], X[:, c, :], ACT.Square).then_inc(sem("n10_sq"), 1)
            root("n10", 1)
            shifted("n10", 0, 24, H)
            for b in range(4):
                act.wait_ge(sem("u2_tr"), b + 1)
                nc.scalar.copy(U2T[:, b // 2, (b % 2) * 512:(b % 2 + 1) * 512], banks[4 + b][:, :]).then_inc(sem("u2_out"), 1)
            for t in range(2):
                act.wait_ge(sem("top"), t + 1)
                nc.scalar.activation(SR[1][:, 32 * t:32 * t + 32], SR[2][:, 32 * t:32 * t + 32], ACT.Exp,
                                     bias=SR[5][:, 4 + t:5 + t]).then_inc(sem("gate_exp"), 1)

            def spread(n):
                for b in range(2):
                    act.wait_ge(sem("gathered"), n * 2 + (b + 1))
                    nc.scalar.copy(XGT[:, 4 * b:4 * b + 4, :], tiles(banks[4 + b][:, :], 4)).then_inc(sem("xgt"), 1)

            def sigmoid(n, c):
                act.wait_ge(sem("up_read"), n * 8 + (2 * c + 5))
                act.wait_ge(sem("act"), n * 4 + (c + 1))
                nc.scalar.activation(SGM[:, c % 2, :], GL[:, c % 2, :], ACT.Sigmoid, scale=1.702).then_inc(sem("sig"), 1)

            def body(n):
                sigmoid(n, 0)
                sigmoid(n, 1)
                act.wait_ge(sem("selg_t"), n + 2)
                act.wait_ge(sem("scattered"), n * 4 + 4)
                nc.scalar.copy(SGT, banks[4][:, 0:256]).then_inc(sem("sgt"), 1)
                sigmoid(n, 2)
                sigmoid(n, 3)
                spread(n + 1)
                act.wait_ge(sem("down"), n * 4 + 4)
                for b in range(2):
                    act.wait_ge(sem("act_t"), n * 2 + (b + 3))
                    nc.scalar.copy(ACTT[:, 4 * b:4 * b + 4, :], tiles(banks[6 + b][:, :], 4)).then_inc(sem("act_out"), 1)
                act.wait_ge(sem("down"), n * 4 + 8)
                for b in range(2):
                    nc.scalar.copy(YE[:, 512 * b:512 * b + 512], banks[2 + b][:, :]).then_inc(sem("ye"), 1)

            spread(0)
            passes(act, body)
            square("n11", lambda c: X[:, c, :], "n11_x")
            root("n11", 0)

        @block.vector
        def _(dve):
            me = Steps(dve, sem("dve_steps"))
            V = nc.vector

            def rstd(name, half):
                dve.wait_ge(sem(name + "_root"), before(name + "_root") + 1)
                r = RS[:, half * T:(half + 1) * T]
                me(V.reciprocal(r, r))
                return r

            def normed(name, r, gain, dst=H):
                for c in range(KT):
                    V.scalar_tensor_tensor(dst[:, c, :], X[:, c, :], par_col(*gain(c)), r, ALU.mult,
                                           ALU.mult).then_inc(sem(name + "_h"), 1)

            def residual(name, r, y, gain):
                t = tiles(TMP, 4)
                for c in range(KT + 1):
                    if c < KT:
                        if c >= 4:
                            dve.wait_ge(sem(name + "_x"), before(name + "_x") + c - 3)
                        me.do(V.scalar_tensor_tensor(t[:, c % 4, :], y(c), par_col(*gain(c)), r, ALU.mult, ALU.mult))
                    if c:
                        me.ended(me.n - (c < KT))
                        V.tensor_tensor(X[:, c - 1, :], X[:, c - 1, :], t[:, (c - 1) % 4, :], ALU.add)\
                         .then_inc(sem(name + "_x"), 1)

            def ffn_in(layer):
                name = f"ffn{layer}_in"
                for j in range(FT + 1):
                    if j < FT:
                        u = FIRST_UNIT[name] + j
                        for back in (1, 2):
                            for half, buf in ((0, F_CA), (1, F_CG)):
                                if back == 1:
                                    dve.wait_ge(sem(f"ffn{layer}_tap"), before(f"ffn{layer}_tap") + 2 * j + 2)
                                else:
                                    me.ended(me.n - 1 + half)
                                c = half * FT + j
                                o = buf[:, j % 2, back:T]
                                ins = V.scalar_tensor_tensor(
                                    o, half_of(u, half)[:, 0:T - back],
                                    par_col("ffn_dw", (layer * 3 + 2 - back) * 44 + c), o, ALU.mult, ALU.add)
                                if back == 1:
                                    me.do(ins)
                                else:
                                    ins.then_inc(read_sem(u), 1)
                    if j >= 1:
                        dve.wait_ge(sem(f"ffn{layer}_silu"), before(f"ffn{layer}_silu") + j)
                        V.tensor_tensor(F_ACT[:, j - 1, :], F_CA[:, (j - 1) % 2, :], F_SG[:, (j - 1) % 2, :],
                                        ALU.mult).then_inc(sem(f"ffn{layer}_act"), 1)

            def attention():
                mask = C("mask", 1152)
                dve.wait_ge(sem("tables_in"), 16)

                def masked(h):
                    S, sm = A_S[h % 2], A_SM[h % 2]
                    dve.wait_ge(sem("att_scores"), h + 1)
                    if h >= 2:
                        dve.wait_ge(sem("att_exp"), 2 * (h - 1))
                    for a, b in ((0, 512), (512, 768), (768, 1024), (1024, 1152)):
                        V.scalar_tensor_tensor(S[:, a:b], banks[WORK + a // 512][:, a % 512:a % 512 + b - a],
                                               SCALE_A, mask[:, a:b], ALU.mult, ALU.add)\
                         .then_inc(sem("att_masked"), 1)
                    for i, (a, b) in enumerate(((0, 768), (768, 1152))):
                        dve.wait_ge(sem("att_masked"), 4 * h + 2 * i + 2)
                        me.do(V.tensor_reduce(sm[:, i:i + 1], S[:, a:b], AX.X, ALU.max))
                    for i in range(2):
                        me.ended(me.n - 1 + i)
                        V.tensor_scalar(sm[:, 2 + i:3 + i], sm[:, i:i + 1], -1.0, None, ALU.mult)\
                         .then_inc(sem("att_max"), 1)

                def scaled(h):
                    Pm, sm = A_P[h % 2], A_SM[h % 2]
                    for i, (a, b) in enumerate(((0, 768), (768, 1152))):
                        dve.wait_ge(sem("att_exp"), 2 * h + i + 1)
                        me(V.reciprocal(sm[:, 6 + i:7 + i], sm[:, 4 + i:5 + i]))
                        V.tensor_scalar(Pm[:, a:b], Pm[:, a:b], sm[:, 6 + i:7 + i], None, ALU.mult)\
                         .then_inc(sem("att_p"), 1)

                masked(0)
                for h in range(HEADS):
                    scaled(h)
                    if h + 1 < HEADS:
                        masked(h + 1)

            me(V.memset(ONE_COL, 1.0))
            V.memset(EPS_COL, EPS).then_inc(sem("eps_set"), 1)
            me(V.memset(G[:, :, 0:TAPS - 1], 0.0))
            dve.wait_ge(sem("x_in"), 16)
            dve.wait_ge(sem("par_in"), 16)
            dve.wait_ge(sem("con_in"), 16)
            normed("n0", rstd("n0", 0), lambda c: ("mix_pre", c))

            def conv(c):
                for k in range(TAPS):
                    for i in range(2):
                        w, src = par_col("cm_dw", k * 8 + c + i), G[:, c + i, k:k + T]
                        if k == 0:
                            me.do(V.tensor_scalar(U[:, c + i, :], src, w, par_col("cm_dw_b", c + i),
                                                  ALU.mult, ALU.add))
                            continue
                        me.ended(me.n - 1 if k < TAPS - 1 else me.n - 1 + i)
                        ins = V.scalar_tensor_tensor(U[:, c + i, :], src, w, U[:, c + i, :], ALU.mult, ALU.add)
                        if k < TAPS - 1:
                            me.do(ins)
                        else:
                            ins.then_inc(sem("conv"), 1)

            for j in range(8):
                unit_half(dve, FIRST_UNIT["cm_in"] + j, 2)
                V.tensor_tensor(G[:, j, TAPS - 1:], G[:, j, TAPS - 1:], SG[:, j, :], ALU.mult).then_inc(sem("glu"), 1)
                if j in (1, 3, 7):
                    dve.wait_ge(sem("glu"), j + 1)
                    conv(min(j - 1, 4))
            dve.wait_ge(sem("conv_pe"), 1)
            for c in (6, 7):
                V.tensor_scalar(U[:, c, :], banks[WORK + 1][:, (c - 6) * T:(c - 5) * T], par_col("cm_dw_b", c), None,
                                ALU.add).then_inc(sem("conv"), 1)
            dve.wait_ge(sem("ln_mean"), 1)
            for c in range(KT):
                V.tensor_tensor(U[:, c, :], U[:, c, :], banks[WORK][:, 0:T], ALU.subtract)\
                 .then_inc(sem("ln_centred"), 1)
            r = rstd("ln", 1)
            for c in range(KT):
                V.tensor_tensor(U[:, c, :], U[:, c, :], r, ALU.mult).then_inc(sem("ln_scaled"), 1)
            units_read(dve, "cm_out")
            residual("n1", rstd("n1", 0), lambda c: Y[:, c, :], lambda c: ("mix_post", c))
            normed("n2", rstd("n2", 1), lambda c: ("ffn_pre", c))
            ffn_in(0)
            residual("n3", rstd("n3", 0), acc, lambda c: ("ffn_post", c))
            r = rstd("n4", 1)
            normed("n4", r, lambda c: ("kv_norm", c))
            normed("n5", r, lambda c: ("mix_pre", 8 + c), SQ)
            for i in range(1, 36, 2):
                u = FIRST_UNIT["kv"] + i
                unit_ready(dve, u)
                for j in range(2):
                    V.tensor_copy(kvq(i, j), half_of(u, j)).then_inc(read_sem(u), 1)
            attention()
            units_read(dve, "o")
            residual("n6", rstd("n6", 0), lambda c: Y[:, c, :], lambda c: ("mix_post", 8 + c))
            normed("n7", rstd("n7", 1), lambda c: ("ffn_pre", 8 + c))
            ffn_in(1)
            unit_half(dve, FIRST_UNIT["ada3"], 2)
            for v in range(2):
                me(V.tensor_tensor(MOD[:, 0:16, v], MOD[:, 0:16, v], par[:, PAR["ada_b"]:PAR["ada_b"] + 16], ALU.add))
                me(V.scalar_tensor_tensor(GS1[:, :, v], MOD[:, 8:16, v], 1.0, par[:, PAR["norm1"]:PAR["norm1"] + 8],
                                          ALU.add, ALU.mult))
            dve.wait_ge(sem("rows_in"), 16)
            lam = rows[:, 0:256].rearrange("p (a b d) -> p a b d", a=2, b=2)
            me(V.tensor_tensor(tiles(LW, 2), lam[:, :, 0, :], lam[:, :, 1, :], ALU.mult))
            V.tensor_reduce(LAM[:, 0:2], tiles(LW, 2), AX.X, ALU.add).then_inc(sem("lam_dot"), 1)
            residual("n8", rstd("n8", 0), acc, lambda c: ("ffn_post", 8 + c))

            def modulated(name, r, src, gain, dst):
                for c in range(KT):
                    V.scalar_tensor_tensor(dst[:, c, :], src[:, c, :], gain(c), r, ALU.mult, ALU.mult)\
                     .then_inc(sem(name + "_p"), 1)

            def take(first, last):
                for i in range(first, last):
                    if i % 2:
                        u, dst = second[i]
                        unit_ready(dve, u)
                        for j in range(2):
                            V.tensor_copy(dst[j], half_of(u, j)).then_inc(read_sem(u), 1)

            modulated("nc", rstd("nc", 1), CT, lambda c: GS1[:, c, 1:2], UC)
            modulated("n9", rstd("n9", 0), X, lambda c: GS1[:, c, 0:1], H)
            dve.wait_ge(sem("lam_exp"), 1)
            me(V.tensor_tensor(LAM[:, 4:5], LAM[:, 2:3], LAM[:, 3:4], ALU.subtract))
            me(V.tensor_scalar(LAM[:, 5:6], LAM[:, 4:5], -1.0, -LAM_INIT, ALU.mult, ALU.add))
            take(0, 2)
            dve.wait_ge(sem("gates"), 1)
            me(V.tensor_tensor(GT, tiles(banks[4][:, 0:64], 4),
                               rows[:, 256:272].unsqueeze(1).to_broadcast([P, 4, 16]), ALU.add))
            gates = GT.rearrange("p t (d i h) -> p t d i h", d=2, i=2)
            dh = lambda a: a.rearrange("p t (d h) -> p t d h", d=2)
            for d in range(2):
                ins = V.scalar_tensor_tensor(dh(AB)[:, :, d, :], gates[:, :, d, 1, :], -1.0, gates[:, :, d, 1, :],
                                             ALU.mult, ALU.max)
                me(ins) if d == 0 else ins.then_inc(sem("abs_f"), 1)
            dve.wait_ge(sem("f_ln"), 1)
            for d in range(2):
                ins = V.scalar_tensor_tensor(dh(LF)[:, :, d, :], gates[:, :, d, 1, :], 0.0, dh(AB)[:, :, d, :],
                                             ALU.min, ALU.subtract)
                me(ins) if d == 0 else ins.then_inc(sem("logf"), 1)
            take(2, 6)
            dve.wait_ge(sem("cumf"), 1)
            me(V.tensor_copy(BT, tiles(banks[5][:, 0:32], 4)))
            for d in range(2):
                ins = V.tensor_tensor(dh(RR)[:, :, d, :], gates[:, :, d, 0, :], dh(BT)[:, :, d, :], ALU.subtract)
                me(ins) if d == 0 else ins.then_inc(sem("rr"), 1)
            take(6, 14)
            dve.wait_ge(sem("rr_t"), 1)
            V.tensor_copy(RT, banks[6][0:8, :]).then_inc(sem("rt"), 1)
            take(14, 26)
            dve.wait_ge(sem("n9_p"), before("n9_p") + KT)
            for i in range(8):
                take(26 + i, 27 + i)
                r = i // 4
                for c in (2 * (i % 4), 2 * (i % 4) + 1):
                    x = DQ[:, c, :] if r == 0 else DK[:, c, T:]
                    t = RS[:, (c % 2) * T:(c % 2 + 1) * T]
                    dve.wait_ge(sem("turned"), 4 * r + c // 2 + 1)
                    if r or c >= 2:
                        dve.wait_ge(sem("rope"), 8 * r + c - 1)
                    me.do(V.tensor_tensor(t, acc(c), C("sin", 256), ALU.mult))
                    me(V.tensor_tensor(x, x, C("cos", 256), ALU.mult))
                    V.tensor_tensor(x, x, t, ALU.add).then_inc(sem("rope"), 1)

            dve.wait_ge(sem("mmask_in"), 16)
            four = lambda a: a.rearrange("p (q d) -> p q d", q=2)
            for h in range(4):
                dve.wait_ge(sem("m_scores"), h + 1)
                if h:
                    dve.wait_ge(sem("m_p"), 2 * h)
                for i in range(4):
                    me.do(V.tensor_tensor(ME[:, i, :], banks[6 + i % 2][:, :], MMASK[:, i, :], ALU.add))
                for i in range(4):
                    me.ended(me.n - 3)
                    me.do(V.tensor_reduce(MX[:, i:i + 1], ME[:, i, :], AX.X, ALU.max))
                me.ended()
                me(V.tensor_scalar(NM, MX, 0.0, -1.0, ALU.max, ALU.mult))
                V.tensor_tensor(four(BM), four(NM), dh(BT)[:, 2:4, :, h], ALU.subtract).then_inc(sem("m_nm"), 1)
                for i in range(4):
                    dve.wait_ge(sem("m_exp"), 5 * h + i + 1)
                    me.do(V.scalar_tensor_tensor(ME[:, i, :], ME[:, i, :], SCALE_M, banks[4 + i // 2][:, :],
                                                 ALU.mult, ALU.mult, accum_out=DEN[:, i:i + 1]))
                me.ended()
                dve.wait_ge(sem("m_exp"), 5 * h + 5)
                me(V.scalar_tensor_tensor(REC, DEN, -1.0, EXM, ALU.mult, ALU.max))
                me(V.tensor_tensor(REC, REC, DEN, ALU.max))
                me(V.reciprocal(REC, REC))
                if h:
                    dve.wait_ge(sem("m_tr"), 2 * h)
                for q in range(2):
                    me.do(V.tensor_scalar(MP[:, q, :], ME[:, 2 * q, :], REC[:, 2 * q:2 * q + 1], None, ALU.mult))
                for q in range(2):
                    me.ended(me.n - 1 + q)
                    V.scalar_tensor_tensor(MP[:, q, :], ME[:, 2 * q + 1, :], REC[:, 2 * q + 1:2 * q + 2], MP[:, q, :],
                                           ALU.mult, ALU.add).then_inc(sem("m_p"), 1)

            def d_max(h):
                b = h % 2
                for i in range(4):
                    dve.wait_ge(sem("d_scores"), 4 * h + i + 1)
                    me.do(V.tensor_reduce(DMX[b][:, i:i + 1], banks[4 + i][:, :], AX.X, ALU.max))
                me.ended()
                V.tensor_scalar(DNM[b], DMX[b], -SCALE_D, None, ALU.mult).then_inc(sem("d_nm"), 1)

            d_max(0)
            for h in range(HEADS):
                b = h % 2
                dve.wait_ge(sem("d_exp"), 4 * h + 4)
                me(V.reciprocal(DREC[b], DDEN[b]))
                me(V.tensor_scalar(DREC[b][:, 2:4], DREC[b][:, 2:4], LAM[:, 5:6], None, ALU.mult))
                for q in range(2):
                    me.do(V.tensor_scalar(DP[b][:, q, :], DP[b][:, q, :], DREC[b][:, q:q + 1], None, ALU.mult))
                for q in range(2):
                    me.ended(me.n - 1 + q)
                    V.scalar_tensor_tensor(DP[b][:, q, :], DP[b][:, 2 + q, :], DREC[b][:, 2 + q:3 + q], DP[b][:, q, :],
                                           ALU.mult, ALU.add).then_inc(sem("d_a"), 1)
                if h + 1 < HEADS:
                    d_max(h + 1)

            units_read(dve, "ada6")
            me(V.tensor_tensor(MOD[:, 16:48, 0], MOD[:, 16:48, 0], par[:, PAR["ada_b"] + 16:PAR["ada_b"] + 48], ALU.add))
            me(V.scalar_tensor_tensor(GS2, MOD[:, 32:40, 0], 1.0, par[:, PAR["norm2"]:PAR["norm2"] + 8], ALU.add, ALU.mult))
            dve.wait_ge(sem("hm_root"), 2)
            for b in range(2):
                me.do(V.reciprocal(RSM[:, 512 * b:512 * b + 512], RSM[:, 512 * b:512 * b + 512]))
            me.ended()
            units_read(dve, "go")
            for c in range(KT + 1):
                if c < KT:
                    me.do(V.scalar_tensor_tensor(HM[:, c, :], HM[:, c, :], par_col("m_norm", c),
                                                 RSM[:, (c // 2) * T:(c // 2 + 1) * T], ALU.mult, ALU.mult))
                if c:
                    me.ended(me.n - (c < KT))
                    V.tensor_tensor(HM[:, c - 1, :], HM[:, c - 1, :], GO[:, c - 1, :], ALU.mult).then_inc(sem("a_out"), 1)
            dve.wait_ge(sem("do_root"), 4)
            for b in range(4):
                r = RSD[:, 512 * b:512 * b + 512]
                me.do(V.reciprocal(r, r))
            for b in range(4):
                r = RSD[:, 512 * b:512 * b + 512]
                me.ended(me.n - 3)
                me.do(V.tensor_scalar(r, r, 1.0 - LAM_INIT, None, ALU.mult))
            me.ended()
            for c in range(KT):
                V.scalar_tensor_tensor(DO[:, c, :], DO[:, c, :], par_col("d_norm", c), RSD[:, c * T:(c + 1) * T],
                                       ALU.mult, ALU.mult).then_inc(sem("b_out"), 1)
            units_read(dve, "gb")
            for c in range(KT):
                u = FIRST_UNIT["wa"] + c // 2
                unit_ready(dve, u)
                V.tensor_tensor(YM[:, c, :], GA[:, c, :], half_of(u, c % 2), ALU.mult).then_inc(read_sem(u), 1)
            units_read(dve, "wa")
            t = tiles(TMP, 4)
            for c in range(KT):
                u = FIRST_UNIT["wb"] + c // 2
                unit_ready(dve, u)
                if c >= 4:
                    dve.wait_ge(sem("ym"), c - 3)
                V.tensor_tensor(t[:, c % 4, :], GB[:, c, :], half_of(u, c % 2), ALU.mult).then_inc(read_sem(u), 1)
                unit_half(dve, u, c % 2 + 1)
                V.tensor_tensor(YM[:, c, :], YM[:, c, :], t[:, c % 4, :], ALU.add).then_inc(sem("ym"), 1)
            for c in range(KT):
                u = FIRST_UNIT["wo"] + c // 2
                unit_ready(dve, u)
                V.scalar_tensor_tensor(X[:, c, :], half_of(u, c % 2), MOD[:, 16 + c, 0:1], X[:, c, :], ALU.mult, ALU.add)\
                 .then_inc(read_sem(u), 1)
            units_read(dve, "wo")
            modulated("n10", rstd("n10", 1), X, lambda c: GS2[:, c:c + 1], H)

            me.do(V.memset(POSA[:, :, :], -1.0))
            me.do(V.memset(GATA[:, :, :], 0.0))
            me(V.memset(SR[3][:, 32:64], 1.0))
            dve.wait_ge(sem("logits"), 1)
            me(V.tensor_tensor(tiles(SR[2], 2), tiles(banks[0][:, 0:64], 2),
                               rows[:, 272:304].unsqueeze(1).to_broadcast([P, 2, EXPERTS]), ALU.add))
            for t in range(2):
                at = slice(32 * t, 32 * t + 32)
                logit, best = SR[2][:, at], SR[3][:, 8 * t:8 * t + 8]
                me(V.max(best, logit))
                V.tensor_scalar(SR[5][:, 4 + t:5 + t], best[:, 0:1], -1.0, None, ALU.mult).then_inc(sem("top"), 1)
                me.do(V.tensor_scalar(SR[4][:, at], logit, best[:, 3:4], None, ALU.is_gt))
                me(V.tensor_scalar(SR[6][:, at], logit, best[:, 3:4], None, ALU.is_equal))
                me(V.tensor_reduce(SR[5][:, t:t + 1], SR[4][:, at], AX.X, ALU.add))
                me.do(V.tensor_scalar(SR[5][:, 2 + t:3 + t], SR[5][:, t:t + 1], -1.0, float(TOP_K), ALU.mult, ALU.add))
                me(V.tensor_tensor_scan(SR[7][:, at], SR[3][:, 32:64], SR[6][:, at], 0.0, ALU.mult, ALU.add))
                me(V.scalar_tensor_tensor(SR[8][:, at], SR[7][:, at], SR[5][:, 2 + t:3 + t], SR[6][:, at],
                                          ALU.is_le, ALU.mult))
                V.tensor_tensor(SR[0][:, at], SR[4][:, at], SR[8][:, at], ALU.add).then_inc(sem("chosen"), 1)
            for t in range(2):
                at = slice(32 * t, 32 * t + 32)
                dve.wait_ge(sem("chosen"), t + 1)
                dve.wait_ge(sem("gate_exp"), t + 1)
                me(V.scalar_tensor_tensor(SR[7][:, at], SR[1][:, at], 1.0, SR[0][:, at], ALU.mult, ALU.mult,
                                          accum_out=SR[5][:, 6 + t:7 + t]))
                me(V.reciprocal(SR[5][:, 8 + t:9 + t], SR[5][:, 6 + t:7 + t]))
                V.tensor_scalar(SR[1][:, at], SR[7][:, at], SR[5][:, 8 + t:9 + t], None, ALU.mult)\
                 .then_inc(sem("gate_w"), 1)
            dve.wait_ge(sem("places"), 1)
            full = SR[5][:, 16:17]
            me(V.tensor_reduce(full, banks[1][:, 64:96], AX.X, ALU.max))
            me(V.tensor_scalar(SR[5][:, 17:18], full, float(CAP), None, ALU.is_gt))
            me(V.scalar_tensor_tensor(SR[5][:, 18:19], full, 2.0 * CAP, SR[5][:, 17:18], ALU.is_gt, ALU.add))
            V.scalar_tensor_tensor(NEXT, full, 3.0 * CAP, SR[5][:, 18:19], ALU.is_gt, ALU.add).then_inc(sem("extra"), 1)
            for t in range(2):
                me.do(V.scalar_tensor_tensor(SR[8][:, 32 * t:32 * t + 32], banks[1][:, 32 * t:32 * t + 32], 1.0,
                                             SR[0][:, 32 * t:32 * t + 32], ALU.add, ALU.mult))
            me.ended()
            for r in range(4):
                me.do(V.tensor_scalar(POSA[:, :, 32 * r:32 * r + 32], tiles(SR[8], 2), -1.0 - CAP * r, None, ALU.add))
                if r == 0:
                    dve.wait_ge(sem("gate_w"), 2)
                me.do(V.tensor_copy(GATA[:, :, 32 * r:32 * r + 32], tiles(SR[1], 2)))
            dve.wait_ge(sem("gate_t"), 1)
            V.tensor_copy(GTT, banks[2][0:EXPERTS, 0:256]).then_inc(sem("gtt"), 1)
            me.ended()

            moe = Steps(dve, sem("moe_steps"))

            def select(to, cols, weight=None, signal=None):
                for t in range(2):
                    for e in range(2):
                        ins = V.tensor_scalar(to[:, t, e * CAP:(e + 1) * CAP], C("slot", CAP), POSC[:, t, cols + e:cols + e + 1],
                                              weight[:, t, e:e + 1] if weight is not None else None, ALU.is_equal,
                                              ALU.mult if weight is not None else ALU.bypass)
                        if t and e:
                            ins.then_inc(sem(signal), 1)

            def one_hot(p):
                for e in range(2):
                    V.tensor_copy(ONEH[:, e * CAP:(e + 1) * CAP], ident[0:EXPERTS, bass.ds(p * 2 + e, 1)]
                                  .to_broadcast([EXPERTS, CAP])).then_inc(sem("hot"), 1)

            me(V.tensor_copy(POSC[:, :, 2:4], POSA[:, :, 0:2]))
            select(SEL, 2, signal="sel")
            one_hot(0)
            for b in range(4):
                dve.wait_ge(sem("b2_done"), b + 1)
                V.tensor_copy(YACC[:, 2 * b:2 * b + 2, :], tiles(banks[4 + b][:, :], 2)).then_inc(sem("b2_read"), 1)
            V.memset(YE, 0.0).then_inc(sem("ye"), 1)
            V.memset(SGT, 0.0).then_inc(sem("sgt"), 1)
            dve.sem_inc(sem("up_read"), 4)
            dve.sem_inc(sem("act"), 2)
            dve.sem_inc(sem("scat_read"), 2)
            dve.sem_inc(sem("moe_steps"), 1)
            dve.wait_ge(sem("b2_read"), 4)
            dve.wait_ge(sem("sel"), 1)
            MOE_STEPS = 6

            def add_scattered(n):
                dve.wait_ge(sem("scat_read"), n * 4 + 2)
                for j in range(4):
                    dve.wait_ge(sem("scattered"), n * 4 + (j + 1))
                    V.tensor_tensor(YACC[:, 2 * j:2 * j + 2, :], YACC[:, 2 * j:2 * j + 2, :],
                                    tiles(banks[6 + j % 2][:, :], 2), ALU.add).then_inc(sem("scat_read"), 1)

            def body(n):
                moe.n, moe.base = 0, n * MOE_STEPS + 1
                dve.wait_ge(sem("sel"), n + 1)
                moe.ended(0)
                moe.do(V.tensor_copy(POSC, POSA[:, :, bass.ds(n * 2, 4)]))
                moe.do(V.tensor_copy(GATC, GATA[:, :, bass.ds(n * 2, 2)]))
                moe.ended()
                dve.wait_ge(sem("selg_t"), n + 1)
                select(SELG, 0, GATC, "selg")
                dve.wait_ge(sem("gathered"), n * 2 + 2)
                select(SEL, 2, signal="sel")
                for c in range(4):
                    glu, lin, sig = GL[:, c % 2, :], LN[:, c % 2, :], SGM[:, c % 2, :]
                    bank = banks[c % 2][:, :].rearrange("p (i g n) -> p i g n", i=2, g=2)
                    dve.wait_ge(sem("act"), n * 4 + (c + 1))
                    dve.wait_ge(sem("up"), n * 8 + (2 * c + 2))
                    V.tensor_scalar(tiles(glu, 2), bank[:, :, 0, :], 7.0, None, ALU.min).then_inc(sem("up_read"), 1)
                    V.tensor_scalar(tiles(lin, 2), bank[:, :, 1, :], 7.0, -7.0, ALU.min, ALU.max)\
                     .then_inc(sem("up_read"), 1)
                    dve.wait_ge(sem("up_read"), n * 8 + (2 * c + 6))
                    moe(V.scalar_tensor_tensor(lin, lin, 1.0, glu, ALU.add, ALU.mult))
                    dve.wait_ge(sem("sig"), n * 4 + (c + 1))
                    if c == 0:
                        dve.wait_ge(sem("act_t"), n * 2 + 2)
                    V.tensor_tensor(ACTS[:, c, :], lin, sig, ALU.mult).then_inc(sem("act"), 1)
                    if c == 1:
                        add_scattered(n)
                dve.wait_ge(sem("up"), n * 8 + 8)
                one_hot((n + 1) % PAIRS)
                assert moe.n == MOE_STEPS

            passes(dve, body)
            n_end = total_pairs(dve)
            add_scattered(n_end)
            dve.wait_ge(sem("scat_read"), n_end * 4 + 6)
            for c in range(KT):
                V.scalar_tensor_tensor(X[:, c, :], YACC[:, c, :], MOD[:, 40 + c, 0:1], X[:, c, :], ALU.mult, ALU.add)\
                 .then_inc(sem("n11_x"), 1)
            normed("n11", rstd("n11", 0), lambda c: ("final", c))


def slabs(w, halves=1):
    n = w.shape[1] // 256
    return w.reshape(KT, P, halves, n, 256 // halves).transpose(3, 1, 0, 2, 4).reshape(n, P, SLAB)


def columns(a):
    return np.ascontiguousarray(a).reshape(-1, P).T


def kernel(**inputs):
    import concourse.bacc as bacc
    from concourse.bass_utils import run_bass_kernel_spmd

    a = {k: np.asarray(v) for k, v in inputs.items()}

    ada = slabs(a["ada_w_2"][0])
    w = a["w_in_2"][0]
    splits = np.cumsum([512, 512, 1024, 16, 1024, 1024, 1024, 1024, 1024])
    mq, mk, mv, mg, go, dq, dk, dv, ga, gb = np.split(w, splits, axis=1)
    weights = {
        "cm_in": slabs(a["cm_w_in"][0], 2), "cm_out": slabs(a["cm_w_out"][0]),
        "kv": slabs(a["w_kv"]), "q": slabs(a["w_q"][0]), "o": slabs(a["w_o"][0]),
        "mq": slabs(mq), "mk": slabs(mk), "mv": slabs(mv), "dq": slabs(dq), "dk": slabs(dk), "dv": slabs(dv),
        "go": slabs(go), "ga": slabs(ga), "gb": slabs(gb),
        "wa": slabs(a["w_branch_a_2"][0]), "wb": slabs(a["w_branch_b_2"][0]), "wo": slabs(a["w_out_2"][0]),
    }
    for i in range(2):
        weights[f"ffn{i}_in"] = slabs(a["ffn_w_in"][i], 2)
        weights[f"ffn{i}_out"] = a["ffn_w_out"][i].reshape(FT // 2, 2, P, D).transpose(0, 2, 1, 3)\
            .reshape(FT // 2, P, SLAB)
    dense, n = [], 0
    for name, k, _ in SCHEDULE:
        if name.startswith("ada"):
            dense.append(ada[n:n + k])
            n += k
        else:
            dense.append(weights[name])
    dense = np.concatenate(dense)
    experts = np.empty((PAIRS, 12, 2, P, SLAB), np.float32)
    experts[:, :8] = a["exp_w1_2"][0].reshape(PAIRS, 2, KT, P, 2, 8, P).transpose(0, 5, 1, 3, 2, 4, 6)\
        .reshape(PAIRS, 8, 2, P, SLAB)
    experts[:, 8:] = a["exp_w2_2"][0].reshape(PAIRS, 2, 4, 2, P, D).transpose(0, 2, 1, 4, 3, 5)\
        .reshape(PAIRS, 4, 2, P, SLAB)

    par = np.concatenate([columns(v) for v in (
        a["mix_pre_g"], a["mix_post_g"], a["ffn_pre_g"], a["ffn_post_g"], a["cm_b_in"], a["cm_dw"], a["cm_dw_b"],
        a["cm_ln_g"], a["cm_ln_b"], a["cm_b_out"], a["kv_norm_g"], a["ffn_dw"], a["ffn_dw_b"], a["c_2"],
        a["c_ctx_2"], a["ada_b_2"], a["norm1_g_2"], a["norm2_g_2"], a["mlstm_norm_g_2"], a["diff_norm_g_2"],
        a["final_norm_g_2"])], axis=1)
    rows = np.concatenate([a["diff_lambda_2"].reshape(-1), a["mlstm_gate_b_2"].reshape(-1),
                           a["router_b_2"].reshape(-1)])
    feature_major = lambda x: x.T.reshape(KT, P, -1).transpose(1, 0, 2)
    arrays = {
        "x": feature_major(a["x"][0]), "ctx": feature_major(a["ctx_2"][0]), "par": par, "con": constants(), "mmask": mlstm_masks(),
        "rows": np.broadcast_to(rows, (P, NROW)), "gatew": mg.reshape(KT, P, 16).transpose(1, 0, 2),
        "routerw": a["router_w_2"][0].reshape(KT, P, EXPERTS).transpose(1, 0, 2), "b1": a["exp_b1_2"][0].reshape(EXPERTS, 2, KT, P).transpose(0, 2, 1, 3).reshape(EXPERTS, 2048),
        "b2": a["exp_b2_2"][0],
        "dense": dense, "experts": experts.reshape(EXPERTS * 12, P, SLAB),
    }
    arrays = {k: np.ascontiguousarray(v) for k, v in arrays.items()}
    nc = bacc.Bacc("TRN2", target_bir_lowering=False, num_devices=1)
    args = [nc.dram_tensor("in_" + k, v.shape, F32, kind="ExternalInput").ap() for k, v in arrays.items()]
    args.append(nc.dram_tensor("out", (P, KT, T), F32, kind="ExternalOutput").ap())
    build(nc, *args)
    r = run_bass_kernel_spmd(nc, [{"in_" + k: v for k, v in arrays.items()}], core_ids=[0])
    out = r.results[0]["out"]
    return out.transpose(2, 1, 0).reshape(1, T, D)
```
